# Optimizing a Trainium2 kernel written in Bass

```python
import jax, jax.numpy as jnp
from jax import lax
import numpy as np
import math

D_MODEL = 1024
BATCH = 1
SEQ = 512
DEPTH = 2

CHUNK = 64
Q_BLOCK = 128
N_A_LAYERS = DEPTH // 2
N_B_LAYERS = DEPTH - N_A_LAYERS
CONV_WIDTH = 31
D_FF = 4 * D_MODEL
N_HEADS = 8
QK_NOPE_DIM = 128
QK_ROPE_DIM = 64
QK_HEAD_DIM = QK_NOPE_DIM + QK_ROPE_DIM
V_HEAD_DIM = 128
Q_LORA_RANK = 384
KV_LORA_RANK = 256
ROPE_BASE = 10000.0
RMS_EPS = 1e-6
LN_EPS = 1e-5


def rms_norm(x, g):
    xf = x.astype(jnp.float32)
    y = xf * lax.rsqrt(jnp.mean(xf * xf, axis=-1, keepdims=True) + RMS_EPS)
    return (y * g.astype(jnp.float32)).astype(x.dtype)

def layer_norm(x, g, b):
    xf = x.astype(jnp.float32)
    mu = jnp.mean(xf, axis=-1, keepdims=True)
    xc = xf - mu
    var = jnp.mean(xc * xc, axis=-1, keepdims=True)
    y = xc * lax.rsqrt(var + LN_EPS) * g.astype(jnp.float32) + b.astype(jnp.float32)
    return y.astype(x.dtype)

def rope_tables(seq):
    inv = 1.0 / (ROPE_BASE ** (jnp.arange(0, QK_ROPE_DIM, 2, dtype=jnp.float32) / QK_ROPE_DIM))
    pos = jnp.arange(seq, dtype=jnp.float32)
    ang = pos[:, None] * inv[None, :]
    return jnp.cos(ang), jnp.sin(ang)

def apply_rope(x, cos, sin):
    xf = x.astype(jnp.float32)
    half = QK_ROPE_DIM // 2
    x1, x2 = xf[..., :half], xf[..., half:]
    out = jnp.concatenate([x1 * cos - x2 * sin, x1 * sin + x2 * cos], axis=-1)
    return out.astype(x.dtype)

def conformer_conv(h, w_pw1, b_pw1, w_dw, b_dw, ln_g, ln_b, w_pw2, b_pw2):
    u = h @ w_pw1 + b_pw1
    a, gate = jnp.split(u, 2, axis=-1)
    u = a * jax.nn.sigmoid(gate)
    u = jnp.pad(u, ((0, 0), (CONV_WIDTH - 1, 0), (0, 0)))
    u = lax.conv_general_dilated(u, w_dw[:, None, :], window_strides=(1,), padding='VALID',
                                 dimension_numbers=('NWC', 'WIO', 'NWC'),
                                 feature_group_count=D_MODEL) + b_dw
    u = jax.nn.silu(layer_norm(u, ln_g, ln_b))
    return u @ w_pw2 + b_pw2

def squared_relu_mlp(h, w1, w2):
    return jnp.square(jax.nn.relu(h @ w1)) @ w2

def mla_shared_kv(h, kv_in_g, w_dkv, kv_norm_g, w_kr, w_uk, w_uv, cos, sin):
    b, s, _ = h.shape
    hn = rms_norm(h, kv_in_g)
    c_kv = rms_norm(hn @ w_dkv, kv_norm_g)
    k_rope = apply_rope(hn @ w_kr, cos, sin)
    k_nope = (c_kv @ w_uk).reshape(b, s, N_HEADS, QK_NOPE_DIM)
    v = (c_kv @ w_uv).reshape(b, s, N_HEADS, V_HEAD_DIM)
    return k_nope, k_rope, v

def mla_attention(hn, w_dq, q_norm_g, w_uq, w_o, k_nope, k_rope, v, cos, sin):
    b, s, _ = hn.shape
    q = (rms_norm(hn @ w_dq, q_norm_g) @ w_uq).reshape(b, s, N_HEADS, QK_HEAD_DIM)
    q_nope = q[..., :QK_NOPE_DIM]
    q_rope = apply_rope(q[..., QK_NOPE_DIM:], cos[:, None, :], sin[:, None, :])
    scale = QK_HEAD_DIM ** -0.5
    key_chunk = jnp.arange(s) // CHUNK

    def block(i):
        start = i * Q_BLOCK
        qn = lax.dynamic_slice_in_dim(q_nope, start, Q_BLOCK, axis=1)
        qr = lax.dynamic_slice_in_dim(q_rope, start, Q_BLOCK, axis=1)
        sc = (jnp.einsum('bqhd,bkhd->bhqk', qn, k_nope, preferred_element_type=jnp.float32)
              + jnp.einsum('bqhr,bkr->bhqk', qr, k_rope, preferred_element_type=jnp.float32)) * scale
        q_chunk = (start + jnp.arange(Q_BLOCK)) // CHUNK
        mask = key_chunk[None, :] <= q_chunk[:, None]
        sc = jnp.where(mask[None, None], sc, -jnp.inf)
        p = jax.nn.softmax(sc, axis=-1).astype(v.dtype)
        return jnp.einsum('bhqk,bkhd->bqhd', p, v)

    o = lax.map(block, jnp.arange(s // Q_BLOCK))
    o = jnp.transpose(o, (1, 0, 2, 3, 4)).reshape(b, s, N_HEADS * V_HEAD_DIM)
    return o @ w_o

def first_inputs(seed: int = 0) -> dict:
    key = jax.random.key(seed)
    ks = jax.random.split(key, 40)
    f32 = jnp.float32

    def nrm(k, shape, fan_in):
        return jax.random.normal(k, shape, f32) * (fan_in ** -0.5)

    def gain(k, shape):
        return 1.0 + 0.1 * jax.random.normal(k, shape, f32)

    def bias(k, shape):
        return 0.02 * jax.random.normal(k, shape, f32)

    D = D_MODEL
    return {
        "x": jax.random.normal(ks[0], (BATCH, SEQ, D), f32),
        "mix_pre_g": gain(ks[1], (DEPTH, D)),
        "mix_post_g": gain(ks[2], (DEPTH, D)),
        "ffn_pre_g": gain(ks[3], (DEPTH, D)),
        "ffn_post_g": gain(ks[4], (DEPTH, D)),
        "w_ff1": nrm(ks[5], (DEPTH, D, D_FF), D),
        "w_ff2": nrm(ks[6], (DEPTH, D_FF, D), D_FF),
        "conv_w_pw1": nrm(ks[7], (N_A_LAYERS, D, 2 * D), D),
        "conv_b_pw1": bias(ks[8], (N_A_LAYERS, 2 * D)),
        "conv_w_dw": nrm(ks[9], (N_A_LAYERS, CONV_WIDTH, D), CONV_WIDTH),
        "conv_b_dw": bias(ks[10], (N_A_LAYERS, D)),
        "conv_ln_g": gain(ks[11], (N_A_LAYERS, D)),
        "conv_ln_b": bias(ks[12], (N_A_LAYERS, D)),
        "conv_w_pw2": nrm(ks[13], (N_A_LAYERS, D, D), D),
        "conv_b_pw2": bias(ks[14], (N_A_LAYERS, D)),
        "mla_w_dq": nrm(ks[15], (N_B_LAYERS, D, Q_LORA_RANK), D),
        "mla_q_norm_g": gain(ks[16], (N_B_LAYERS, Q_LORA_RANK)),
        "mla_w_uq": nrm(ks[17], (N_B_LAYERS, Q_LORA_RANK, N_HEADS * QK_HEAD_DIM), Q_LORA_RANK),
        "mla_w_o": nrm(ks[18], (N_B_LAYERS, N_HEADS * V_HEAD_DIM, D), N_HEADS * V_HEAD_DIM),
        "kv_in_g": gain(ks[19], (D,)),
        "kv_w_dkv": nrm(ks[20], (D, KV_LORA_RANK), D),
        "kv_norm_g": gain(ks[21], (KV_LORA_RANK,)),
        "kv_w_kr": nrm(ks[22], (D, QK_ROPE_DIM), D),
        "kv_w_uk": nrm(ks[23], (KV_LORA_RANK, N_HEADS * QK_NOPE_DIM), KV_LORA_RANK),
        "kv_w_uv": nrm(ks[24], (KV_LORA_RANK, N_HEADS * V_HEAD_DIM), KV_LORA_RANK),
    }

def first_block(x, mix_pre_g, mix_post_g, ffn_pre_g, ffn_post_g, w_ff1, w_ff2,
              conv_w_pw1, conv_b_pw1, conv_w_dw, conv_b_dw, conv_ln_g, conv_ln_b,
              conv_w_pw2, conv_b_pw2, mla_w_dq, mla_q_norm_g, mla_w_uq, mla_w_o,
              kv_in_g, kv_w_dkv, kv_norm_g, kv_w_kr, kv_w_uk, kv_w_uv):
    cos, sin = rope_tables(x.shape[1])
    h = x
    k_nope = k_rope = v = None
    for layer in range(DEPTH):
        if layer == N_A_LAYERS:
            k_nope, k_rope, v = mla_shared_kv(h, kv_in_g, kv_w_dkv, kv_norm_g, kv_w_kr,
                                              kv_w_uk, kv_w_uv, cos, sin)
        hn = rms_norm(h, mix_pre_g[layer])
        if layer < N_A_LAYERS:
            a = layer
            m = conformer_conv(hn, conv_w_pw1[a], conv_b_pw1[a], conv_w_dw[a], conv_b_dw[a],
                               conv_ln_g[a], conv_ln_b[a], conv_w_pw2[a], conv_b_pw2[a])
        else:
            bl = layer - N_A_LAYERS
            m = mla_attention(hn, mla_w_dq[bl], mla_q_norm_g[bl], mla_w_uq[bl], mla_w_o[bl],
                              k_nope, k_rope, v, cos, sin)
        h = h + rms_norm(m, mix_post_g[layer])
        f = squared_relu_mlp(rms_norm(h, ffn_pre_g[layer]), w_ff1[layer], w_ff2[layer])
        h = h + rms_norm(f, ffn_post_g[layer])
    return h


DEPTH_2 = 1

DN_HEADS = 4
DN_HEAD_DIM = 128
DN_WIDTH = DN_HEADS * DN_HEAD_DIM
DN_QKV_WIDTH = 3 * DN_WIDTH
DN_CONV = 4
DN_CHUNK = 64
SWA_HEADS = 8
SWA_KV_HEADS = 2
SWA_HEAD_DIM = 64
SWA_GROUP = SWA_HEADS // SWA_KV_HEADS
SWA_WIDTH = SWA_HEADS * SWA_HEAD_DIM
SWA_KV_WIDTH = SWA_KV_HEADS * SWA_HEAD_DIM
WINDOW = 128
SWA_BLOCK = 128
REL_BUCKETS = 32
REL_MAX_DIST = 128
N_BRANCHES = 2
D_FF_2 = ((8 * D_MODEL // 3 + 255) // 256) * 256
D_IN = DN_QKV_WIDTH + DN_WIDTH + 2 * DN_HEADS + SWA_WIDTH + 2 * SWA_KV_WIDTH + N_BRANCHES * D_MODEL
EPS = 1e-6


def rms_norm_2(x, gain):
    xf = x.astype(jnp.float32)
    y = xf * lax.rsqrt(jnp.mean(xf * xf, axis=-1, keepdims=True) + EPS)
    return (y * gain.astype(jnp.float32)).astype(x.dtype)

def l2_norm(x):
    xf = x.astype(jnp.float32)
    return xf * lax.rsqrt(jnp.sum(xf * xf, axis=-1, keepdims=True) + EPS)

def causal_dwconv(x, w):
    k = w.shape[0]
    return lax.conv_general_dilated(
        x, w[:, None, :], window_strides=(1,), padding=((k - 1, 0),),
        dimension_numbers=("NWC", "WIO", "NWC"), feature_group_count=x.shape[-1])

def chunk_gated_delta_rule(q, k, v, g, beta):
    B, S, H, DK = q.shape
    DV = v.shape[-1]
    C = DN_CHUNK
    NC = S // C
    q = q * (DK ** -0.5)

    def to_chunks(t):
        return t.reshape(B, NC, C, H, t.shape[-1]).transpose(0, 3, 1, 2, 4)

    qc, kc, vc = to_chunks(q), to_chunks(k), to_chunks(v)
    gc = jnp.cumsum(g.reshape(B, NC, C, H).transpose(0, 3, 1, 2), axis=-1)
    bc = beta.reshape(B, NC, C, H).transpose(0, 3, 1, 2)[..., None]
    k_beta = kc * bc
    v_beta = vc * bc

    idx = jnp.arange(C)
    lower_incl = idx[:, None] >= idx[None, :]
    strict_lower = idx[:, None] > idx[None, :]
    decay = jnp.exp(jnp.where(lower_incl, gc[..., :, None] - gc[..., None, :], -jnp.inf))

    a_mat = jnp.where(strict_lower, jnp.einsum("bhncd,bhnsd->bhncs", k_beta, kc) * decay, 0.0)
    lhs = a_mat + jnp.eye(C, dtype=a_mat.dtype)
    rhs = jnp.concatenate([v_beta, k_beta * jnp.exp(gc)[..., None]], axis=-1)
    sol = lax.linalg.triangular_solve(lhs, rhs, left_side=True, lower=True, unit_diagonal=True)
    u, w = sol[..., :DV], sol[..., DV:]
    qk = jnp.einsum("bhncd,bhnsd->bhncs", qc, kc) * decay

    def step(state, inp):
        q_i, k_i, u_i, w_i, g_i, qk_i = inp
        v_new = u_i - jnp.einsum("bhck,bhkv->bhcv", w_i, state)
        o_i = (jnp.einsum("bhck,bhkv->bhcv", q_i * jnp.exp(g_i)[..., None], state)
               + jnp.einsum("bhcs,bhsv->bhcv", qk_i, v_new))
        g_last = g_i[..., -1]
        k_dec = k_i * jnp.exp(g_last[..., None] - g_i)[..., None]
        state = state * jnp.exp(g_last)[..., None, None] + jnp.einsum("bhck,bhcv->bhkv", k_dec, v_new)
        return state, o_i

    xs = tuple(jnp.moveaxis(t, 2, 0) for t in (qc, kc, u, w, gc, qk))
    state0 = jnp.zeros((B, H, DK, DV), jnp.float32)
    _, o = lax.scan(step, state0, xs)
    return o.transpose(1, 0, 3, 2, 4).reshape(B, S, H, DV)

def gated_deltanet_branch(qkv, z, b_raw, a_raw, conv_w, a_log, dt_bias, out_gain):
    B, S, _ = qkv.shape
    qkv = jax.nn.silu(causal_dwconv(qkv, conv_w))
    q, k, v = jnp.split(qkv, 3, axis=-1)
    q = l2_norm(q.reshape(B, S, DN_HEADS, DN_HEAD_DIM))
    k = l2_norm(k.reshape(B, S, DN_HEADS, DN_HEAD_DIM))
    v = v.reshape(B, S, DN_HEADS, DN_HEAD_DIM).astype(jnp.float32)
    beta = jax.nn.sigmoid(b_raw.astype(jnp.float32))
    g = -jnp.exp(a_log.astype(jnp.float32)) * jax.nn.softplus(a_raw.astype(jnp.float32) + dt_bias.astype(jnp.float32))
    o = chunk_gated_delta_rule(q, k, v, g, beta)
    o = rms_norm_2(o, out_gain) * jax.nn.silu(z.reshape(B, S, DN_HEADS, DN_HEAD_DIM).astype(jnp.float32))
    return o.reshape(B, S, DN_WIDTH).astype(qkv.dtype)

def t5_causal_bucket(dist):
    n = jnp.maximum(dist, 0)
    max_exact = REL_BUCKETS // 2
    nf = jnp.maximum(n, 1).astype(jnp.float32)
    large = max_exact + (jnp.log(nf / max_exact) / math.log(REL_MAX_DIST / max_exact)
                         * (REL_BUCKETS - max_exact)).astype(jnp.int32)
    large = jnp.minimum(large, REL_BUCKETS - 1)
    return jnp.where(n < max_exact, n, large)

def sliding_window_branch(q, k, v, q_gain, k_gain, sinks, rel_bias):
    B, S, _ = q.shape
    NB = S // SWA_BLOCK
    q = rms_norm_2(q.reshape(B, S, SWA_HEADS, SWA_HEAD_DIM), q_gain)
    k = rms_norm_2(k.reshape(B, S, SWA_KV_HEADS, SWA_HEAD_DIM), k_gain)
    v = v.reshape(B, S, SWA_KV_HEADS, SWA_HEAD_DIM)
    qb = q.reshape(B, NB, SWA_BLOCK, SWA_KV_HEADS, SWA_GROUP, SWA_HEAD_DIM).astype(jnp.float32)

    def band(t):
        tp = jnp.pad(t, ((0, 0), (SWA_BLOCK, 0), (0, 0), (0, 0)))
        tp = tp.reshape(B, NB + 1, SWA_BLOCK, SWA_KV_HEADS, SWA_HEAD_DIM)
        return jnp.concatenate([tp[:, :-1], tp[:, 1:]], axis=2).astype(jnp.float32)

    kb, vb = band(k), band(v)
    logits = jnp.einsum("bnqkgd,bnskd->bnkgqs", qb, kb) * (SWA_HEAD_DIM ** -0.5)

    qi = jnp.arange(SWA_BLOCK)[:, None]
    kj = jnp.arange(2 * SWA_BLOCK)[None, :]
    dist = SWA_BLOCK + qi - kj
    in_window = (dist >= 0) & (dist < WINDOW)
    key_pos = (jnp.arange(NB)[:, None] - 1) * SWA_BLOCK + jnp.arange(2 * SWA_BLOCK)[None, :]
    mask = in_window[None, :, :] & (key_pos >= 0)[:, None, :]

    bias = rel_bias.astype(jnp.float32)[t5_causal_bucket(dist)]
    bias = bias.transpose(2, 0, 1).reshape(SWA_KV_HEADS, SWA_GROUP, SWA_BLOCK, 2 * SWA_BLOCK)
    logits = jnp.where(mask[None, :, None, None], logits + bias, -jnp.inf)

    sink = sinks.astype(jnp.float32).reshape(SWA_KV_HEADS, SWA_GROUP)[None, None, :, :, None, None]
    m = jnp.maximum(jnp.max(logits, axis=-1, keepdims=True), sink)
    p = jnp.exp(logits - m)
    denom = jnp.sum(p, axis=-1, keepdims=True) + jnp.exp(sink - m)
    out = jnp.einsum("bnkgqs,bnskd->bnqkgd", p / denom, vb)
    return out.reshape(B, S, SWA_WIDTH).astype(q.dtype)

def split_combined(p):
    sizes = (DN_QKV_WIDTH, DN_WIDTH, DN_HEADS, DN_HEADS, SWA_WIDTH, SWA_KV_WIDTH, SWA_KV_WIDTH,
             N_BRANCHES * D_MODEL)
    return jnp.split(p, np.cumsum(sizes)[:-1].tolist(), axis=-1)

def second_inputs(seed: int = 0) -> dict:
    key = jax.random.key(seed)
    ks = jax.random.split(key, 20)
    f32 = jnp.float32
    L = DEPTH_2

    def nrm(k, shape, scale):
        return jax.random.normal(k, shape, f32) * scale

    dt = jnp.exp(jax.random.uniform(ks[5], (L, DN_HEADS), f32, math.log(1e-3), math.log(1e-1)))
    return {
        "x": nrm(ks[0], (BATCH, SEQ, D_MODEL), 1.0),
        "attn_norm": 1.0 + nrm(ks[1], (L, D_MODEL), 0.02),
        "w_in": nrm(ks[2], (L, D_MODEL, D_IN), D_MODEL ** -0.5),
        "dn_conv": nrm(ks[3], (L, DN_CONV, DN_QKV_WIDTH), DN_CONV ** -0.5),
        "dn_a_log": jnp.log(jax.random.uniform(ks[4], (L, DN_HEADS), f32, 1.0, 16.0)),
        "dn_dt_bias": dt + jnp.log(-jnp.expm1(-dt)),
        "dn_out_norm": 1.0 + nrm(ks[6], (L, DN_HEAD_DIM), 0.02),
        "swa_q_norm": 1.0 + nrm(ks[7], (L, SWA_HEAD_DIM), 0.02),
        "swa_k_norm": 1.0 + nrm(ks[8], (L, SWA_HEAD_DIM), 0.02),
        "swa_sinks": nrm(ks[9], (L, SWA_HEADS), 0.5),
        "rel_bias": nrm(ks[10], (REL_BUCKETS, SWA_HEADS), 0.1),
        "w_branch_dn": nrm(ks[11], (L, DN_WIDTH, D_MODEL), DN_WIDTH ** -0.5),
        "w_branch_swa": nrm(ks[12], (L, SWA_WIDTH, D_MODEL), SWA_WIDTH ** -0.5),
        "w_out": nrm(ks[13], (L, D_MODEL, D_MODEL), D_MODEL ** -0.5),
        "ffn_norm": 1.0 + nrm(ks[14], (L, D_MODEL), 0.02),
        "w_gate": nrm(ks[15], (L, D_MODEL, D_FF_2), D_MODEL ** -0.5),
        "w_up": nrm(ks[16], (L, D_MODEL, D_FF_2), D_MODEL ** -0.5),
        "w_down": nrm(ks[17], (L, D_FF_2, D_MODEL), D_FF_2 ** -0.5),
    }

def second_block(x, attn_norm, w_in, dn_conv, dn_a_log, dn_dt_bias, dn_out_norm, swa_q_norm,
              swa_k_norm, swa_sinks, rel_bias, w_branch_dn, w_branch_swa, w_out, ffn_norm,
              w_gate, w_up, w_down):
    B, S, _ = x.shape
    for l in range(DEPTH_2):
        h = rms_norm_2(x, attn_norm[l])
        proj = h @ w_in[l]
        dn_qkv, dn_z, dn_b, dn_a, sq, sk, sv, gate_raw = split_combined(proj)
        y_dn = gated_deltanet_branch(dn_qkv, dn_z, dn_b, dn_a, dn_conv[l], dn_a_log[l],
                                     dn_dt_bias[l], dn_out_norm[l])
        y_swa = sliding_window_branch(sq, sk, sv, swa_q_norm[l], swa_k_norm[l], swa_sinks[l], rel_bias)
        gates = jax.nn.sigmoid(gate_raw.astype(jnp.float32)).astype(x.dtype)
        gates = gates.reshape(B, S, N_BRANCHES, D_MODEL)
        merged = gates[:, :, 0] * (y_dn @ w_branch_dn[l]) + gates[:, :, 1] * (y_swa @ w_branch_swa[l])
        x = x + merged @ w_out[l]
        h2 = rms_norm_2(x, ffn_norm[l])
        x = x + (jax.nn.silu(h2 @ w_gate[l]) * (h2 @ w_up[l])) @ w_down[l]
    return x


def setup_inputs(seed=0):
    out = dict(first_inputs(seed))
    for name, value in second_inputs(seed + 1).items():
        if name != "x":
            out[name + "_2"] = value
    return out


def reference(
    x, mix_pre_g, mix_post_g, ffn_pre_g, ffn_post_g, w_ff1, w_ff2, conv_w_pw1, conv_b_pw1,
    conv_w_dw, conv_b_dw, conv_ln_g, conv_ln_b, conv_w_pw2, conv_b_pw2, mla_w_dq, mla_q_norm_g,
    mla_w_uq, mla_w_o, kv_in_g, kv_w_dkv, kv_norm_g, kv_w_kr, kv_w_uk, kv_w_uv, attn_norm_2,
    w_in_2, dn_conv_2, dn_a_log_2, dn_dt_bias_2, dn_out_norm_2, swa_q_norm_2, swa_k_norm_2,
    swa_sinks_2, rel_bias_2, w_branch_dn_2, w_branch_swa_2, w_out_2, ffn_norm_2, w_gate_2,
    w_up_2, w_down_2,
):
    x = first_block(
        x, mix_pre_g, mix_post_g, ffn_pre_g, ffn_post_g, w_ff1, w_ff2, conv_w_pw1, conv_b_pw1,
        conv_w_dw, conv_b_dw, conv_ln_g, conv_ln_b, conv_w_pw2, conv_b_pw2, mla_w_dq,
        mla_q_norm_g, mla_w_uq, mla_w_o, kv_in_g, kv_w_dkv, kv_norm_g, kv_w_kr, kv_w_uk,
        kv_w_uv,
    )
    return second_block(
        x, attn_norm_2, w_in_2, dn_conv_2, dn_a_log_2, dn_dt_bias_2, dn_out_norm_2,
        swa_q_norm_2, swa_k_norm_2, swa_sinks_2, rel_bias_2, w_branch_dn_2, w_branch_swa_2,
        w_out_2, ffn_norm_2, w_gate_2, w_up_2, w_down_2,
    )


_drawn_inputs = setup_inputs


def setup_inputs(seed=0):
    import zlib

    import numpy as np

    out = dict(_drawn_inputs(seed))
    spreads = {}
    factors = {'conv_b_pw1': 2.763,
     'conv_ln_b': 2.687,
     'mla_q_norm_g': 3.72,
     'attn_norm_2': 8.0,
     'dn_out_norm_2': 8.0,
     'swa_q_norm_2': 8.0,
     'swa_k_norm_2': 8.0,
     'swa_sinks_2': 200.0,
     'rel_bias_2': 23.291,
     'ffn_norm_2': 7.877}
    for name, (base, spread) in spreads.items():
        noise = np.random.default_rng([zlib.crc32(name.encode()), seed]).standard_normal(out[name].shape)
        drawn = base * np.exp(spread * noise) if base else spread * noise
        out[name] = __import__('jax').numpy.asarray(drawn.astype(out[name].dtype))
    for name, factor in factors.items():
        out[name] = (out[name] * factor).astype(out[name].dtype)
    return out
```

```python
import math
from contextlib import ExitStack

import concourse.bass as bass
from concourse import mybir
from concourse.alu_op_type import AluOpType as ALU

F32 = mybir.dt.float32
F32R = mybir.dt.float32r
ACT = mybir.ActivationFunctionType
AX_X = mybir.AxisListType.X

P = 128
SEQ = 512
TT = SEQ // P
D = 1024
DT = D // P
D_FF = 4096
FF_BLOCKS = D_FF // D
TAPS = 31
PAD = TAPS - 1
NH, NOPE, ROPE, QKD = 8, 128, 64, 192
Q_LORA, KV_LORA = 384, 256
DN_H, DN_TAPS, DN_CH = 4, 4, 64
SW_H, SW_D = 8, 64
D_FF2 = 2816
FF2_TILES = (8, 8, 6)
CW = 2048
RMS_EPS, LN_EPS = 1e-6, 1e-5
BIG = 1e30
ROPE_BASE = 10000.0
BUCKETS, MAX_DIST = 32, 128
RELW = 3 * P

CONST_COLS = {}
_at = 0
for _name, _n in (("ident", P), ("ones", P), ("half_ones", P), ("inv_mask", 6 * P),
                  ("decay_mask", P), ("decay_mask_t", P), ("tri", P), ("rev", P)):
    CONST_COLS[_name] = (_at, _at + _n)
    _at += _n
N_CONST = _at

COLS = {}
_at = 2
for _name, _n in (("max", 8), ("neg_max", 8), ("row_sum", 8), ("inv_sum", 8), ("sink_exp", 8),
                  ("ba", 8 * TT), ("beta", DN_H * TT), ("dt_in", DN_H * TT), ("decay", DN_H * TT),
                  ("abs_in", DN_H * TT), ("soft", DN_H * TT), ("cum", DN_H * TT), ("cum_exp", DN_H * TT),
                  ("beta_exp", DN_H * TT), ("rev_exp", DN_H * TT), ("a_log", DN_H), ("dt_bias", DN_H),
                  ("sinks", SW_H), ("a_exp", DN_H), ("rel", SW_H)):
    COLS[_name] = (_at, _at + _n)
    _at += _n
N_COLS = _at

VEC = {}
_at = 0
for _name, _n in (("mix_pre", 16), ("mix_post", 16), ("ffn_pre", 16), ("ffn_post", 16), ("b_pw1", 16),
                  ("b_dw", 8), ("ln_g", 8), ("ln_b", 8), ("b_pw2", 8), ("q_norm", 3), ("kv_in", 8),
                  ("kv_norm", 2), ("attn_norm", 8), ("dn_out", 1), ("ffn_norm", 8), ("swa_q", 1),
                  ("swa_k", 1), ("w_dw", 8 * TAPS), ("dn_conv", 12 * DN_TAPS)):
    VEC[_name] = _at
    _at += _n
N_VEC = _at

START, WIDTH = {}, []
for _name, _w in (("pw1", [CW] * 8), ("pw2", [CW] * 4), ("ffn_0", [CW] * 32), ("latent", [CW] * 3),
                  ("uk", [512] * 4), ("uq", [768] * 6), ("uv", [512] * 4), ("wo", [CW] * 4),
                  ("ffn_1", [CW] * 32), ("ba", [64]), ("sq", [CW] * 2), ("sk", [CW]), ("sv", [1024]),
                  ("qkv", [CW] * 6), ("z", [CW] * 2), ("merge", [CW, CW, 1024, 1024] * 4),
                  ("w_out", [CW] * 4), ("ffn_2", [CW] * 30 + [1536] * 4)):
    START[_name] = len(WIDTH)
    WIDTH += _w
N_CHUNK = len(WIDTH)

STAGES = ([("mix0_pre", 8, 8), ("ln", 8, 8), ("mix0_post", 8, 8), ("ffn0_pre", 8, 8), ("ffn0_post", 8, 8),
           ("mla_in", 8, 16), ("kv", 2, 2), ("q", 3, 3), ("mix1_post", 8, 8), ("ffn1_pre", 8, 8),
           ("ffn1_post", 8, 8), ("attn2", 8, 8)] + [(f"swa_q{i}", 1, 1) for i in range(4)]
          + [(f"swa_k{i}", 1, 1) for i in range(2)] + [(f"dn_in{i}", 1, 1) for i in range(8)]
          + [(f"dn_out{i}", 1, 1) for i in range(4)] + [("ffn2_pre", 8, 8)])
STAGE_NO, SQUARES0, READS0, SQUARES = {}, {}, {}, {}
_a = _b = 0
for _i, (_name, _n, _r) in enumerate(STAGES):
    STAGE_NO[_name], SQUARES0[_name], READS0[_name], SQUARES[_name] = _i, _a, _b, _n
    _a += _n
    _b += _r

SPLIT0 = {}
_a = 0
for _name, _n in (("mix0_pre", 8), ("ln", 8), ("ffn0_pre", 8), ("mla_kv_in", 8), ("mla_q_in", 8), ("kv", 2),
                  ("q", 3), ("heads", 8), ("ffn1_pre", 8), ("attn2", 8), ("swa", 4), ("dn", 4),
                  ("merged", 8), ("ffn2_pre", 8)):
    SPLIT0[_name] = _a
    _a += _n
RES = {n: 8 * i for i, n in enumerate(("mix0", "ffn0", "mix1", "ffn1", "merge", "out"))}


def runs(first, last):
    found, c = [], first
    while c < last:
        n = 1
        while c + n < last and WIDTH[c + n] == WIDTH[c]:
            n += 1
        found.append((c, n))
        c += n
    return found


def build(nc, A, out, last_chunk=N_CHUNK, upto="out"):
    ctx = ExitStack()
    with ctx:
        def sb(name, shape, dt=F32):
            return ctx.enter_context(nc.sbuf_tensor(name, shape, dt))

        def sem(name):
            return ctx.enter_context(nc.semaphore(name))

        wraw = sb("wraw", [P, 2, CW])
        whi = sb("whi", [P, 2, CW], F32R)
        wlo = sb("wlo", [P, 2, CW], F32R)
        resid = sb("resid", [P, DT, SEQ])
        xh = sb("xh", [P, DT, SEQ], F32R)
        xl = sb("xl", [P, DT, SEQ], F32R)
        hh = sb("hh", [P, DT, SEQ], F32R)
        hl = sb("hl", [P, DT, SEQ], F32R)
        Y = sb("Y", [P, DT, SEQ])
        Z = sb("Z", [P, 16, SEQ])
        E = sb("E", [P, 6, SEQ])
        SQ = sb("SQ", [P, 2, SEQ])
        NT = sb("NT", [P, 2, SEQ])
        K = sb("K", [P, N_CONST])
        PV = sb("PV", [P, N_VEC])
        small = sb("small", [P, N_COLS])
        ps = ctx.enter_context(nc.psum_tensor("ps", [P, 8, SEQ], F32))
        SUMS, ROOT = 4, 5
        SCORE, TURN, OUTPUT = (4, 5, 0, 1), (6, 2), (7, 3)

        def const(name):
            a, b = CONST_COLS[name]
            return K[:, a:b]

        def cols(name):
            a, b = COLS[name]
            return small[:, a:b]

        def col(name, i):
            return small[:, COLS[name][0] + i:COLS[name][0] + i + 1]

        ident, ones, half_ones = map(const, ("ident", "ones", "half_ones"))

        def vec(name, i=0):
            return PV[:, VEC[name] + i:VEC[name] + i + 1]

        eps_rms, eps_ln = small[:, 0:1], small[:, 1:2]
        UW = SEQ + PAD
        U = Z[:, 0:9, :].rearrange("p a b -> p (a b)")[:, 0:DT * UW].rearrange("p (t n) -> p t n", n=UW)

        cos_t, sin_t, rotate = Z[:, 14, :], Z[:, 15, :], Z[:, 13, 0:P]
        V = Z[:, 8:16, :].rearrange("p (t a) n -> p t (a n)", t=TT)
        rope_raw = Z[:, 8:10, :]
        onehot = E[0:BUCKETS + 1, 0, 0:RELW]
        rel_wide = E[0:BUCKETS + 1, 1:3, :].rearrange("p a n -> p (a n)").rearrange("p (h n) -> p h n", n=P)
        rel_rows = [E[:, 3:6, :].rearrange("p a n -> p (a n)").rearrange("p (h n) -> p h n", n=RELW),
                    Z[:, 9:12, :].rearrange("p a n -> p (a n)").rearrange("p (h n) -> p h n", n=RELW)]
        bias = E[:, 0:4, :].rearrange("p a n -> p (a n)").rearrange("p (h n) -> p h n", n=2 * P)
        rel_scratch = nc.dram_tensor("rel_scratch", (SW_H, P, RELW), F32, kind="Internal")
        sv_tok = E[:, 4, :]
        RW = SEQ + DN_TAPS - 1
        raw4 = E[:, 0:5, :].rearrange("p a n -> p (a n)")[:, 0:4 * RW].rearrange("p (a n) -> p a n", n=RW)

        def by_head(t):
            return t.rearrange("p (h n) -> p h n", n=P)

        def bcast_heads(m):
            return m.unsqueeze(1).to_broadcast([P, DN_H, P])

        raw_loaded = [sem("raw_loaded_even"), sem("raw_loaded_odd")]
        hi_ready, lo_ready, chunk_done = sem("hi_ready"), sem("lo_ready"), sem("chunk_done")
        pair_free = [sem("pair_free_even"), sem("pair_free_odd")]
        consts_loaded, x_loaded = sem("consts_loaded"), sem("x_loaded")
        eps_ready, pads_zeroed, y_zeroed = sem("eps_ready"), sem("pads_zeroed"), sem("y_zeroed")
        dve_step, act_step = sem("dve_step"), sem("act_step")
        resid_ready = sem("resid_ready")
        squares_ready, squares_summed = sem("squares_ready"), sem("squares_summed")
        root_ready, root_read = sem("root_ready"), sem("root_read")
        split_hi, split_done = sem("split_hi"), sem("split_done")
        gate_ready, taps_done, conv_ready = sem("gate_ready"), sem("taps_done"), sem("conv_ready")
        mean_summed, centred = sem("mean_summed"), sem("centred")
        hidden_sq, hidden_hi, hidden_ready = map(sem, ("hidden_sq", "hidden_hi", "hidden_ready"))
        out_stored = sem("out_stored")
        tables_loaded, rows_loaded = sem("tables_loaded"), sem("rows_loaded")
        rel_summed, rel_copied, rel_stored, bias_loaded, rel_spread = map(
            sem, ("rel_summed", "rel_copied", "rel_stored", "bias_loaded", "rel_spread"))
        rotated, roped = sem("rotated"), sem("roped")
        scores_ready, max_ready, probs_ready, probs_scaled, probs_turned, probs_back, pv_done = map(
            sem, ("scores_ready", "max_ready", "probs_ready", "probs_scaled", "probs_turned", "probs_back",
                  "pv_done"))
        swa_keys_ready, swa_ready = sem("swa_keys_ready"), sem("swa_ready")
        ba_ready, softplus_in, softplus_out, decay_ready, decay_summed, decay_exps, beta_exp_ready = map(
            sem, ("ba_ready", "softplus_in", "softplus_out", "decay_ready", "decay_summed", "decay_exps",
                  "beta_exp_ready"))
        dn_taps_done, dn_conv_ready, dn_silu_ready = map(sem, ("dn_taps_done", "dn_conv_ready", "dn_silu_ready"))
        spread_ready, rows_summed, products_ready, tokens_turned = map(
            sem, ("spread_ready", "rows_summed", "products_ready", "tokens_turned"))
        row_exp_ready, diffs_ready, decays_ready, a_ready, qk_ready, qe_ready, tok_ready = map(
            sem, ("row_exp_ready", "diffs_ready", "decays_ready", "a_ready", "qk_ready", "qe_ready", "tok_ready"))
        a_turned, at_ready, level_p, level_m, level_qr, level_t, wu_ready, wu_copied = map(
            sem, ("a_turned", "at_ready", "level_p", "level_m", "level_qr", "level_t", "wu_ready", "wu_copied"))
        ws_ready, new_ready, o_ready, o_copied, state_ready = map(
            sem, ("ws_ready", "new_ready", "o_ready", "o_copied", "state_ready"))
        gated_ready, gates_ready, merged_ready, swa_term = map(
            sem, ("gated_ready", "gates_ready", "merged_ready", "swa_term"))

        block = ctx.enter_context(nc.Block())

        def pair(c):
            return 2 * (c % 2)

        def emptied(eng, c, h=0):
            eng.wait_ge(pair_free[c % 2], h + (c // 2 + 1))

        def multiplied(eng, c, h=0):
            eng.wait_ge(chunk_done, h * 2 + (c + 1))

        def resid_at(eng, name):
            return lambda j: eng.wait_ge(resid_ready, RES[name] + j + 1)

        @block.sync
        def _(sp):
            def load(c, h=0):
                p, w = c % 2, WIDTH[c]
                if c >= 2:
                    sp.wait_ge(lo_ready, h * 2 + (c - 1))
                src = A["stream"][c, :, 0:w] if isinstance(h, int) else A["stream"][bass.ds(h * 2 + c, 1), :, 0:w]
                dst = wraw[:, p, 0:w]
                if not isinstance(h, int):
                    src = src.rearrange("a p n -> p (a n)")
                sp.dma_start(dst, src).then_inc(raw_loaded[p], 16)

            for j in range(0, DT, 2):
                sp.dma_start(resid[:, j:j + 2, :], A["x"][:, j:j + 2, :]).then_inc(x_loaded, 16)
            sp.dma_start(K[:, :], A["consts"]).then_inc(consts_loaded, 16)
            sp.dma_start(PV[:, :], A["vecs"]).then_inc(consts_loaded, 16)
            load(0)
            load(1)
            sp.dma_start(onehot, A["onehot"]).then_inc(rows_loaded, 16)
            sp.dma_start(small[0:BUCKETS, COLS["rel"][0]:COLS["rel"][1]], A["rel_bias"]).then_inc(rows_loaded, 16)
            for n in ("a_log", "dt_bias", "sinks"):
                sp.dma_start(cols(n), A[n].partition_broadcast(P)).then_inc(rows_loaded, 16)
            sp.dma_start(Z[:, 13:16, :], A["tables"]).then_inc(tables_loaded, 16)
            for g in range(2):
                sp.wait_ge(rel_copied, 4 * (g + 1))
                sp.dma_start(rel_scratch.ap()[4 * g:4 * g + 4].rearrange("h p n -> p h n"),
                             rel_rows[g]).then_inc(rel_stored, 16)
            for c, n in runs(2, last_chunk):
                if c == START["ba"] + 1:
                    sp.wait_ge(rel_stored, 32)
                    sp.wait_ge(resid_ready, RES["mix1"] + DT)
                    for h in range(SW_H):
                        src = bass.AP(rel_scratch, h * P * RELW + P - 1, [[RELW - 1, P], [1, 2 * P]])
                        sp.dma_start(bias[:, h, :], src).then_inc(bias_loaded, 16)
                if n > 3:
                    with sp.Fori(0, n // 2) as h:
                        load(c, h)
                        load(c + 1, h)
                    if n % 2:
                        load(c + n - 1)
                else:
                    for k in range(n):
                        load(c + k)
            if upto != "out":
                sp.wait_ge(rel_stored, 32)
                if upto == "merge":
                    for k in range(2): emptied(sp, START["ffn_2"] - 1 - k)
                else:
                    sp.wait_ge(resid_ready, RES[upto] + 8)
                sp.dma_start(out, resid[:, :, :]).then_inc(out_stored, 16)
                sp.wait_ge(out_stored, 16)
                return
            for m in range(4):
                emptied(sp, N_CHUNK - 4 + m)
                sp.dma_start(out[:, 2 * m:2 * m + 2, :], resid[:, 2 * m:2 * m + 2, :]).then_inc(out_stored, 16)
            sp.wait_ge(out_stored, 64)

        @block.gpsimd
        def _(pool):
            def rest(c, h=0):
                p, w = c % 2, WIDTH[c]
                pool.wait_ge(hi_ready, h * 2 + (c + 1))
                if c >= 2:
                    pool.wait_ge(chunk_done, h * 2 + (c - 1))
                pool.tensor_tensor(wlo[:, p, 0:w], wraw[:, p, 0:w], whi[:, p, 0:w],
                                   ALU.subtract).then_inc(lo_ready, 1)

            rest(0)
            rest(1)
            for c, n in runs(2, last_chunk):
                if n > 3:
                    with pool.Fori(0, n // 2) as h:
                        rest(c, h)
                        rest(c + 1, h)
                    if n % 2:
                        rest(c + n - 1)
                else:
                    for k in range(n):
                        rest(c + k)

        @block.scalar
        def _(act):
            steps = [0]

            def step(ins):
                steps[0] += 1
                ins.then_inc(act_step, 1)
                act.wait_ge(act_step, steps[0])

            def head(c, h=0):
                if isinstance(h, int) and c + 2 * h >= last_chunk:
                    return
                p = c % 2
                w = WIDTH[c] if isinstance(h, int) else CW
                act.wait_ge(raw_loaded[p], h * 16 + 16 * (c // 2 + 1))
                if c >= 2:
                    act.wait_ge(chunk_done, h * 2 + (c - 1))
                act.activation(whi[:, p, 0:w], wraw[:, p, 0:w], ACT.Copy).then_inc(hi_ready, 1)

            def stats(stage, src, ready, n_feat, eps):
                base = SQUARES0[stage]
                for j in range(SQUARES[stage]):
                    ready(j)
                    if base + j >= 2:
                        act.wait_ge(squares_summed, base + j - 1)
                    act.activation(SQ[:, (base + j) % 2, :], src(j), ACT.Square).then_inc(squares_ready, 1)
                act.wait_ge(squares_summed, base + SQUARES[stage])
                if READS0[stage]:
                    act.wait_ge(root_read, READS0[stage])
                step(act.activation(ps[:, ROOT, :], ps[:, SUMS, :], ACT.Ln, scale=1.0 / n_feat, bias=eps))
                act.activation(ps[:, ROOT, :], ps[:, ROOT, :], ACT.Exp, scale=-0.5).then_inc(root_ready, 1)

            def split_heads(name, dst, n=8, read0=None):
                for j in range(n):
                    act.wait_ge(root_read, (READS0[name] if read0 is None else read0) + j + 1)
                    act.activation(dst(j), NT[:, (SPLIT0[name] + j) % 2, :], ACT.Copy).then_inc(split_hi, 1)

            def root_table():
                act.preload_act_table_set("natural_log_exp_and_others")

            root_table()
            act.wait_ge(eps_ready, 2)
            head(0)
            head(1)
            for h in range(SW_H):
                act.wait_ge(rel_summed, h + 1)
                act.activation(rel_rows[h // 4][:, h % 4, :], ps[:, 6 + h % 2, 0:RELW],
                               ACT.Copy).then_inc(rel_copied, 1)
            stats("mix0_pre", lambda j: resid[:, j, :], lambda j: act.wait_ge(x_loaded, 64), D, eps_rms)
            split_heads("mix0_pre", lambda j: xh[:, j, :])

            c0 = START["pw1"]
            with act.Fori(0, 4) as h:
                for j in range(2):
                    multiplied(act, c0 + j, h)
                    act.activation(SQ[:, j, :], ps[:, 2 * j + 1, :], ACT.Sigmoid,
                                   bias=PV[:, bass.ds(h * 2 + (VEC["b_pw1"] + DT + j), 1)]).then_inc(gate_ready, 1)
                    head(c0 + j + 2, h)
            root_table()
            def conv_centred(j):
                act.wait_ge(centred, j + 1)
            stats("ln", lambda j: Y[:, j, :], conv_centred, D, eps_ln)
            base = SPLIT0["ln"]
            for j in range(DT):
                act.wait_ge(root_read, READS0["ln"] + j + 1)
                if j >= 2:
                    act.wait_ge(split_done, base + j - 1)
                step(act.activation(NT[:, (base + j) % 2, :], Y[:, j, :], ACT.Silu,
                                    scale=vec("ln_g", j), bias=vec("ln_b", j)))
                act.activation(hh[:, j, :], NT[:, (base + j) % 2, :], ACT.Copy).then_inc(split_hi, 1)
            root_table()
            c0 = START["pw2"]
            for c in range(c0, c0 + 4):
                multiplied(act, c)
                for n in range(2):
                    j = 2 * (c - c0) + n
                    ins = act.activation(Y[:, j, :], ps[:, pair(c) + n, :], ACT.Identity, bias=vec("b_pw2", j))
                ins.then_inc(pair_free[c % 2], 1)
                head(c + 2)

            def post(stage, c_last):
                stats(stage, lambda j: Y[:, j, :], lambda j: emptied(act, c_last - 3 + j // 2), D, eps_rms)

            def pre(stage, name):
                stats(stage, lambda j: resid[:, j, :], resid_at(act, name), D, eps_rms)

            def ffn(layer):
                c0 = START[f"ffn_{layer}"]
                with act.Fori(0, FF_BLOCKS) as b:
                    for j in range(8):
                        c = c0 + j
                        p = c % 2
                        multiplied(act, c, b * 4)
                        if j < 4:
                            relu = Z[:, 2 * p:2 * p + 2, :]
                            act.activation(relu, ps[:, 2 * p:2 * p + 2, :], ACT.Relu).then_inc(pair_free[p], 1)
                            act.wait_ge(hidden_sq, b * 4 + (16 * layer + j + 1))
                            act.activation(hh[:, 2 * j:2 * j + 2, :], Z[:, 4 + 2 * p:6 + 2 * p, :],
                                           ACT.Copy).then_inc(hidden_hi, 1)
                        head(c + 2, b * 4)

            post("mix0_post", START["ffn_0"] - 1)
            pre("ffn0_pre", "mix0")
            split_heads("ffn0_pre", lambda j: xh[:, j, :])
            ffn(0)
            post("ffn0_post", START["latent"] - 1)
            if upto == "ffn0": return

            def copy_pair(c, dst):
                multiplied(act, c)
                act.activation(dst, ps[:, pair(c):pair(c) + 2, :], ACT.Copy).then_inc(pair_free[c % 2], 1)

            pre("mla_in", "ffn0")
            split_heads("mla_kv_in", lambda j: xh[:, j, :], read0=READS0["mla_in"])
            split_heads("mla_q_in", lambda j: hh[:, j, :], read0=READS0["mla_in"] + DT)
            c0 = START["latent"]
            for m in range(3):
                copy_pair(c0 + m, E[:, 2 * m:2 * m + 2, :])
                head(c0 + m + 2)
            emptied(act, c0 + 2)
            stats("kv", lambda j: E[:, j, :], lambda j: None, KV_LORA, eps_rms)
            split_heads("kv", lambda j: xh[:, j, :], 2)
            stats("q", lambda j: E[:, 3 + j, :], lambda j: None, Q_LORA, eps_rms)
            split_heads("q", lambda j: xh[:, 2 + j, :], 3)
            for m in range(4):
                copy_pair(START["uk"] + m, Z[:, 2 * m:2 * m + 2, :])
                head(START["uk"] + m + 2)
            for m in range(6):
                copy_pair(START["uq"] + m, Y[:, 2 * m:2 * m + 2, :] if m < 4 else
                          (SQ[:, :, :] if m == 4 else rope_raw))
                head(START["uq"] + m + 2)
            act.wait_ge(roped, 5)
            for m in range(4):
                c = START["uv"] + m
                multiplied(act, c)
                act.activation(V[:, :, m * 256:(m + 1) * 256],
                               ps[:, pair(c):pair(c) + 2, :].rearrange("p b (t n) -> p (b t) n", n=256),
                               ACT.Copy).then_inc(pair_free[c % 2], 1)
                head(c + 2)

            def attend(it0, n_keys, scale, group, split, dst):
                def back(it):
                    nk = n_keys(it - it0)
                    act.wait_ge(probs_turned, it + 1)
                    if it >= 2:
                        act.wait_ge(pv_done, it - 1)
                    act.activation(SQ[:, it % 2, 0:nk], ps[:, TURN[it % 2], 0:nk], ACT.Copy).then_inc(probs_back, 1)

                def output(g):
                    act.wait_ge(pv_done, it0 + group * (g + 1))
                    act.activation(dst(g), ps[:, OUTPUT[g % 2], :], ACT.Copy).then_inc(split_hi, 1)

                for it in range(it0, it0 + 32):
                    k, s = it % 8, ps[:, SCORE[it % 4], 0:n_keys(it - it0)]
                    act.wait_ge(max_ready, it + 1)
                    if it0:
                        act.activation(col("sink_exp", k), col("sinks", (it - it0) // 4), ACT.Exp,
                                       bias=col("neg_max", k))
                    act.activation(s, s, ACT.Exp, scale=scale, bias=col("neg_max", k),
                                   accum_out=col("row_sum", k)).then_inc(probs_ready, 1)
                    if it > it0:
                        back(it - 1)
                    if it - it0 > group and (it - it0) % group == 1:
                        output((it - it0) // group - 1)
                back(it0 + 31)
                output(32 // group - 1)

            attend(0, lambda n: (n % 4 + 1) * P, QKD ** -0.5, 4, "heads", lambda g: hh[:, g, :])
            for m in range(4):
                copy_pair(START["wo"] + m, Y[:, 2 * m:2 * m + 2, :])
                head(START["wo"] + m + 2)
            post("mix1_post", START["ffn_1"] - 1)
            if upto == "mix1": return
            pre("ffn1_pre", "mix1")
            split_heads("ffn1_pre", lambda j: xh[:, j, :])
            ffn(1)
            post("ffn1_post", START["ba"] - 1)
            if upto == "ffn1": return

            pre("attn2", "ffn1")
            split_heads("attn2", lambda j: xh[:, j, :])
            c = START["ba"]
            multiplied(act, c)
            act.activation(cols("ba"), ps[:, pair(c), 0:8 * TT], ACT.Copy).then_inc(pair_free[c % 2], 1)
            head(c + 2)
            emptied(act, c)
            act.wait_ge(rows_loaded, 80)
            ba = cols("ba").rearrange("p (t n) -> p t n", n=8)
            act.activation(cols("beta").rearrange("p (t n) -> p t n", n=DN_H), ba[:, :, 0:DN_H],
                           ACT.Sigmoid).then_inc(ba_ready, 1)
            root_table()
            act.wait_ge(softplus_in, 1)
            step(act.activation(cols("abs_in"), cols("dt_in"), ACT.Abs))
            step(act.activation(cols("soft"), cols("abs_in"), ACT.Exp, scale=-1.0))
            act.activation(cols("soft"), cols("soft"), ACT.Ln, bias=1.0).then_inc(softplus_out, 1)
            act.activation(cols("a_exp"), cols("a_log"), ACT.Exp).then_inc(softplus_out, 1)
            for m in range(2):
                copy_pair(START["sq"] + m, Y[:, 2 * m:2 * m + 2, :])
                head(START["sq"] + m + 2)
            copy_pair(START["sk"], Y[:, 4:8:2, :])
            head(START["sk"] + 2)
            c = START["sv"]
            multiplied(act, c)
            act.activation(sv_tok, ps[:, pair(c), :], ACT.Copy).then_inc(pair_free[c % 2], 1)
            head(c + 2)
            act.wait_ge(decay_summed, 1)
            act.activation(cols("cum"), ps[:, 6, 0:16], ACT.Copy)
            act.activation(cols("cum_exp"), ps[:, 6, 0:16], ACT.Exp)
            act.activation(cols("rev_exp"), ps[:, 6, 16:32], ACT.Exp).then_inc(decay_exps, 1)
            emptied(act, START["sq"] + 1)
            for i in range(4):
                stats(f"swa_q{i}", lambda j: Y[:, i, :], lambda j: None, SW_D, eps_rms)
            for i in range(2):
                stats(f"swa_k{i}", lambda j: Y[:, 4 + 2 * i, :], lambda j: None, SW_D, eps_rms)
            act.wait_ge(root_read, READS0["swa_k1"] + 1)
            attend(32, lambda n: P if n % 4 == 0 else 2 * P, 1.0, 8, "swa", lambda g: hh[:, 4 + g, :])

            def dn_silu(m):
                act.wait_ge(dn_conv_ready, 2 * (m + 1))
                act.activation(Z[:, 2 * m:2 * m + 2, :], Z[:, 2 * m:2 * m + 2, :], ACT.Silu).then_inc(dn_silu_ready, 1)

            for m in range(6):
                c = START["qkv"] + m
                if m >= 2:
                    act.wait_ge(dn_conv_ready, 2 * (m - 1))
                else:
                    act.wait_ge(pads_zeroed, 2)
                copy_pair(c, raw4[:, 2 * (m % 2):2 * (m % 2) + 2, DN_TAPS - 1:RW])
                head(c + 2)
                if m:
                    dn_silu(m - 1)
            for m in range(2):
                c = START["z"] + m
                multiplied(act, c)
                act.activation(Z[:, 12 + 2 * m:14 + 2 * m, :], ps[:, pair(c):pair(c) + 2, :],
                               ACT.Silu).then_inc(pair_free[c % 2], 1)
                head(c + 2)
                if m == 0:
                    dn_silu(5)
            root_table()
            for i in range(8):
                stats(f"dn_in{i}", lambda j: Z[:, i, :], lambda j: act.wait_ge(dn_silu_ready, i // 2 + 1), 1, eps_rms)

            for t in range(TT):
                tok = slice(t * P, (t + 1) * P)
                act.wait_ge(rows_summed, t + 1)
                if t:
                    act.wait_ge(state_ready, 2 * t)
                act.activation(E[:, 1, :], ps[:, 4, :], ACT.Exp).then_inc(row_exp_ready, 1)
                act.wait_ge(diffs_ready, t + 1)
                act.activation(E[:, 2, :], E[:, 2, :], ACT.Exp, scale=-1.0)
                act.activation(E[:, 3, :], E[:, 3, :], ACT.Exp).then_inc(decays_ready, 1)
                act.wait_ge(tokens_turned, t + 1)
                for h in range(DN_H):
                    k, hp = DN_H * t + h, slice(h * P, (h + 1) * P)
                    act.activation(E[:, 4, hp], ps[:, 7, hp], ACT.Copy, scale=col("beta_exp", k))
                    act.activation(Y[:, 0, hp], ps[:, 7, hp], ACT.Copy, scale=col("rev_exp", k))
                    ins = act.activation(E[:, 5, hp], ps[:, 0, hp], ACT.Copy, scale=col("beta", k))
                ins.then_inc(tok_ready, 1)
                act.wait_ge(a_turned, t + 1)
                act.activation(Y[:, 1, :], ps[:, 1, :], ACT.Copy).then_inc(at_ready, 1)
                act.wait_ge(wu_ready, t + 1)
                act.activation(Y[:, 2, :], ps[:, 1, :], ACT.Copy)
                act.activation(Y[:, 5, :], ps[:, 2, :], ACT.Copy).then_inc(wu_copied, 1)
                for cc in range(2):
                    act.wait_ge(o_ready, 2 * t + cc + 1)
                    at = t * P + cc * DN_CH
                    act.activation(Z[:, 0:DN_H, at:at + DN_CH],
                                   ps[:, 5, 0:DN_H * DN_CH].rearrange("p (h n) -> p h n", n=DN_CH),
                                   ACT.Copy).then_inc(o_copied, 1)
            act.wait_ge(o_copied, 2 * TT)
            for i in range(DN_H):
                stats(f"dn_out{i}", lambda j: Z[:, i, :], lambda j: None, P, eps_rms)
                act.wait_ge(gated_ready, i + 1)
                act.activation(hh[:, i, :], NT[:, (SPLIT0["dn"] + i) % 2, :], ACT.Copy).then_inc(split_hi, 1)

            for m in range(4):
                c = START["merge"] + 4 * m
                for i in range(2):
                    multiplied(act, c + i)
                    if m and i == 0:
                        act.wait_ge(merged_ready, m)
                    ins = act.activation(Z[:, 4 + 2 * i:6 + 2 * i, :], ps[:, pair(c + i):pair(c + i) + 2, :],
                                         ACT.Sigmoid).then_inc(pair_free[(c + i) % 2], 1)
                    head(c + i + 2)
                for i in (2, 3):
                    multiplied(act, c + i)
                    head(c + i + 2)
            for m in range(4):
                act.wait_ge(merged_ready, m + 1)
                for j in (2 * m, 2 * m + 1):
                    act.activation(xh[:, j, :], Y[:, j, :], ACT.Copy).then_inc(split_hi, 1)
            root_table()
            for m in range(4):
                multiplied(act, START["w_out"] + m)
                head(START["w_out"] + m + 2)
            if upto == "merge": return
            stats("ffn2_pre", lambda j: resid[:, j, :], lambda j: emptied(act, START["w_out"] + j // 2), D, eps_rms)
            split_heads("ffn2_pre", lambda j: xh[:, j, :])

            def gated_block(c0, n, b=0):
                for j in range(n):
                    c = c0 + j
                    p = c % 2
                    multiplied(act, c, b * 6)
                    act.activation(Z[:, p, :], ps[:, 2 * p, :], ACT.Silu).then_inc(gate_ready, 1)
                    head(c + 2, b * 6)
                    emptied(act, c, b * 6)
                    act.activation(hh[:, j, :], Z[:, 2 + p, :], ACT.Copy).then_inc(hidden_hi, 1)
                for j in range(n, n + 4):
                    multiplied(act, c0 + j, b * 6)
                    head(c0 + j + 2, b * 6)

            with act.Fori(0, 2) as b:
                gated_block(START["ffn_2"], 8, b)
            gated_block(START["ffn_2"] + 24, FF2_TILES[2])

        @block.vector
        def _(dve):
            steps = [0]

            def step(ins):
                steps[0] += 1
                ins.then_inc(dve_step, 1)
                dve.wait_ge(dve_step, steps[0])

            def take_root(stage):
                dve.wait_ge(root_ready, STAGE_NO[stage] + 1)

            def norm_split(name, src, gain, hi, lo, n=8, stage=None, read0=None):
                take_root(stage or name)
                base = SPLIT0[name]

                def rest(j):
                    dve.wait_ge(split_hi, base + j + 1)
                    dve.tensor_tensor(lo(j), NT[:, (base + j) % 2, :], hi(j), ALU.subtract).then_inc(split_done, 1)

                for j in range(n):
                    if base + j >= 2:
                        dve.wait_ge(split_done, base + j - 1)
                    dve.scalar_tensor_tensor(out=NT[:, (base + j) % 2, :], in0=src(j), scalar=gain(j),
                                             in1=ps[:, ROOT, :], op0=ALU.mult, op1=ALU.mult).then_inc(root_read, 1)
                    if j:
                        rest(j - 1)
                rest(n - 1)

            def add_residual(stage, gain):
                take_root(stage)
                base = READS0[stage]

                def add(j):
                    dve.wait_ge(root_read, base + j + 1)
                    dve.tensor_tensor(resid[:, j, :], resid[:, j, :], Y[:, j, :], ALU.add).then_inc(resid_ready, 1)

                for j in range(DT):
                    dve.scalar_tensor_tensor(out=Y[:, j, :], in0=Y[:, j, :], scalar=gain(j), in1=ps[:, ROOT, :],
                                             op0=ALU.mult, op1=ALU.mult).then_inc(root_read, 1)
                    if j:
                        add(j - 1)
                add(DT - 1)

            dve.memset(eps_rms, RMS_EPS).then_inc(eps_ready, 1)
            dve.memset(eps_ln, LN_EPS).then_inc(eps_ready, 1)
            dve.memset(U[:, :, 0:PAD], 0.0).then_inc(pads_zeroed, 1)
            dve.memset(small[BUCKETS:BUCKETS + 1, COLS["rel"][0]:COLS["rel"][1]], 1.0).then_inc(rel_spread, 1)
            dve.wait_ge(rows_loaded, 80)
            dve.wait_ge(rel_spread, 1)
            dve.tensor_copy(rel_wide, small[0:BUCKETS + 1, COLS["rel"][0]:COLS["rel"][1]].unsqueeze(2)
                            .to_broadcast([BUCKETS + 1, SW_H, P])).then_inc(rel_spread, 1)
            dve.wait_ge(consts_loaded, 32)
            dve.wait_ge(pads_zeroed, 1)
            norm_split("mix0_pre", lambda j: resid[:, j, :], lambda j: vec("mix_pre", j),
                       lambda j: xh[:, j, :], lambda j: xl[:, j, :])

            c0 = START["pw1"]
            with dve.Fori(0, 4) as h:
                for j in range(2):
                    t = h * 2 + j
                    dve.wait_ge(gate_ready, h * 2 + (j + 1))
                    dve.scalar_tensor_tensor(out=U[:, bass.ds(t, 1), PAD:UW], in0=ps[:, 2 * j:2 * j + 1, :],
                                             scalar=PV[:, bass.ds(h * 2 + (VEC["b_pw1"] + j), 1)],
                                             in1=SQ[:, j:j + 1, :], op0=ALU.add,
                                             op1=ALU.mult).then_inc(pair_free[j], 1)
                    emptied(dve, c0 + j, h)
                    even, odd = Y[:, bass.ds(t, 1), :], NT[:, j:j + 1, :]
                    for k in range(TAPS):
                        acc = odd if k % 2 else even
                        w = PV[:, bass.ds(h * 2 + (VEC["w_dw"] + k * DT + j), 1)]
                        shifted = U[:, bass.ds(t, 1), k:k + SEQ]
                        if k < 2:
                            ins = dve.tensor_scalar(acc, shifted, w, None, ALU.mult)
                        else:
                            dve.wait_ge(taps_done, h * (2 * TAPS) + (j * TAPS + k - 1))
                            ins = dve.scalar_tensor_tensor(out=acc, in0=shifted, scalar=w, in1=acc,
                                                           op0=ALU.mult, op1=ALU.add)
                        ins.then_inc(taps_done, 1)
                    dve.wait_ge(taps_done, h * (2 * TAPS) + (j + 1) * TAPS)
                    dve.scalar_tensor_tensor(out=even, in0=even, in1=odd, op0=ALU.add, op1=ALU.add,
                                             scalar=PV[:, bass.ds(h * 2 + (VEC["b_dw"] + j), 1)]
                                             ).then_inc(conv_ready, 1)
            dve.wait_ge(mean_summed, 1)
            step(dve.tensor_scalar(NT[:, 0, :], ps[:, SUMS, :], 1.0 / D, None, ALU.mult))
            for j in range(DT):
                dve.tensor_tensor(Y[:, j, :], Y[:, j, :], NT[:, 0, :], ALU.subtract).then_inc(centred, 1)
            take_root("ln")
            dve.wait_ge(centred, DT)
            for j in range(DT):
                dve.tensor_tensor(Y[:, j, :], Y[:, j, :], ps[:, ROOT, :], ALU.mult).then_inc(root_read, 1)
            for j in range(DT):
                dve.wait_ge(split_hi, SPLIT0["ln"] + j + 1)
                dve.tensor_tensor(hl[:, j, :], NT[:, (SPLIT0["ln"] + j) % 2, :], hh[:, j, :],
                                  ALU.subtract).then_inc(split_done, 1)

            def ffn(layer):
                c0 = START[f"ffn_{layer}"]
                dve.wait_ge(resid_ready, RES[f"mix{layer}"] + DT)
                dve.memset(Y[:, :, :], 0.0).then_inc(y_zeroed, 1)
                dve.wait_ge(y_zeroed, layer + 1)
                with dve.Fori(0, FF_BLOCKS) as b:
                    for j in range(8):
                        c = c0 + j
                        p = c % 2
                        if j < 4:
                            emptied(dve, c, b * 4)
                            relu, sq = Z[:, 2 * p:2 * p + 2, :], Z[:, 4 + 2 * p:6 + 2 * p, :]
                            dve.tensor_tensor(sq, relu, relu, ALU.mult).then_inc(hidden_sq, 1)
                            dve.wait_ge(hidden_hi, b * 4 + (16 * layer + j + 1))
                            dve.tensor_tensor(hl[:, 2 * j:2 * j + 2, :], sq, hh[:, 2 * j:2 * j + 2, :],
                                              ALU.subtract).then_inc(hidden_ready, 1)
                        else:
                            multiplied(dve, c, b * 4)
                            y = Y[:, 2 * (j - 4):2 * (j - 4) + 2, :]
                            dve.tensor_tensor(y, y, ps[:, 2 * p:2 * p + 2, :], ALU.add).then_inc(pair_free[p], 1)

            add_residual("mix0_post", lambda j: vec("mix_post", j))
            norm_split("ffn0_pre", lambda j: resid[:, j, :], lambda j: vec("ffn_pre", j),
                       lambda j: xh[:, j, :], lambda j: xl[:, j, :])
            ffn(0)
            add_residual("ffn0_post", lambda j: vec("ffn_post", j))
            if upto == "ffn0": return

            norm_split("mla_kv_in", lambda j: resid[:, j, :], lambda j: vec("kv_in", j), lambda j: xh[:, j, :],
                       lambda j: xl[:, j, :], stage="mla_in")
            norm_split("mla_q_in", lambda j: resid[:, j, :], lambda j: vec("mix_pre", DT + j),
                       lambda j: hh[:, j, :], lambda j: hl[:, j, :], stage="mla_in")
            norm_split("kv", lambda j: E[:, j, :], lambda j: vec("kv_norm", j), lambda j: xh[:, j, :],
                       lambda j: xl[:, j, :], 2)
            norm_split("q", lambda j: E[:, 3 + j, :], lambda j: vec("q_norm", j), lambda j: xh[:, 2 + j, :],
                       lambda j: xl[:, 2 + j, :], 3)

            dve.wait_ge(split_done, SPLIT0["q"] + 3)
            dve.wait_ge(tables_loaded, 16)
            step(dve.memset(E[:, 4:6, :], 0.0))

            def rope(r, src, dsts):
                dve.wait_ge(rotated, r + 1)
                step(dve.tensor_tensor(NT[:, 0, :], ps[:, 6 + r % 2, :], sin_t, ALU.mult))
                step(dve.tensor_tensor(NT[:, 1, :], src, cos_t, ALU.mult))
                for n, (dst, p) in enumerate(dsts):
                    ins = dve.tensor_tensor(dst, NT[p, 0, :], NT[p, 1, :], ALU.add)
                    if n < len(dsts) - 1:
                        step(ins)
                ins.then_inc(roped, 1)
                dve.wait_ge(roped, r + 1)

            rope(0, E[:, 2, :], [(E[0:ROPE, 4, :], slice(0, ROPE)), (E[ROPE:P, 5, :], slice(ROPE, P))])
            for r in range(4):
                rope(r + 1, SQ[:, r, :] if r < 2 else rope_raw[:, r - 2, :], [(E[:, r, :], slice(0, P))])

            def attend(it0, n_keys, group, name):
                def finish(it):
                    k, nk = it % 8, n_keys(it - it0)
                    dve.wait_ge(probs_ready, it + 1)
                    if it0:
                        step(dve.tensor_tensor(col("row_sum", k), col("row_sum", k), col("sink_exp", k), ALU.add))
                    step(dve.reciprocal(col("inv_sum", k), col("row_sum", k)))
                    if it >= 2:
                        dve.wait_ge(probs_turned, it - 1)
                    dve.tensor_scalar(NT[:, it % 2, 0:nk], ps[:, SCORE[it % 4], 0:nk], col("inv_sum", k), None,
                                      ALU.mult).then_inc(probs_scaled, 1)

                def output(g):
                    j = g + (0 if it0 == 0 else 4)
                    dve.wait_ge(split_hi, SPLIT0[name] + g + 1)
                    dve.tensor_tensor(hl[:, j, :], ps[:, OUTPUT[g % 2], :], hh[:, j, :],
                                      ALU.subtract).then_inc(split_done, 1)

                for it in range(it0, it0 + 32):
                    k, n = it % 8, it - it0
                    nk, bank = n_keys(n), SCORE[it % 4]
                    dve.wait_ge(scores_ready, it + 1)
                    if it0 == 0:
                        step(dve.memset(ps[0:DN_CH, bank, nk - DN_CH:nk], -BIG))
                        step(dve.reduce_max(col("max", k), ps[:, bank, 0:nk], AX_X))
                        dve.tensor_scalar(col("neg_max", k), col("max", k), -(QKD ** -0.5), None,
                                          ALU.mult).then_inc(max_ready, 1)
                    else:
                        step(dve.scalar_tensor_tensor(out=ps[:, bank, 0:nk], in0=ps[:, bank, 0:nk],
                                                      scalar=SW_D ** -0.5, in1=bias[:, n // 4, 2 * P - nk:2 * P],
                                                      op0=ALU.mult, op1=ALU.add))
                        step(dve.reduce_max(col("max", k), ps[:, bank, 0:nk], AX_X))
                        dve.tensor_scalar(col("neg_max", k), col("max", k), col("sinks", n // 4), -1.0, ALU.max,
                                          ALU.mult).then_inc(max_ready, 1)
                    if it > it0:
                        finish(it - 1)
                    if it - it0 > group and (it - it0) % group == 2:
                        output((it - it0) // group - 1)
                finish(it0 + 31)
                output(32 // group - 1)

            attend(0, lambda n: (n % 4 + 1) * P, 4, "heads")
            add_residual("mix1_post", lambda j: vec("mix_post", DT + j))
            if upto == "mix1": return
            norm_split("ffn1_pre", lambda j: resid[:, j, :], lambda j: vec("ffn_pre", DT + j),
                       lambda j: xh[:, j, :], lambda j: xl[:, j, :])
            ffn(1)
            add_residual("ffn1_post", lambda j: vec("ffn_post", DT + j))
            if upto == "ffn1": return

            norm_split("attn2", lambda j: resid[:, j, :], lambda j: vec("attn_norm", j),
                       lambda j: xh[:, j, :], lambda j: xl[:, j, :])
            dve.wait_ge(ba_ready, 1)
            ba = cols("ba").rearrange("p (t n) -> p t n", n=8)

            def by_tile(name):
                return cols(name).rearrange("p (t n) -> p t n", n=DN_H)

            def all_tiles(name):
                return cols(name).unsqueeze(1).to_broadcast([P, TT, DN_H])

            dve.tensor_tensor(by_tile("dt_in"), ba[:, :, DN_H:2 * DN_H], all_tiles("dt_bias"),
                              ALU.add).then_inc(softplus_in, 1)
            dve.wait_ge(softplus_out, 2)
            step(dve.scalar_tensor_tensor(out=cols("soft"), in0=cols("dt_in"), scalar=0.0, in1=cols("soft"),
                                          op0=ALU.max, op1=ALU.add))
            dve.scalar_tensor_tensor(out=by_tile("decay"), in0=by_tile("soft"), scalar=-1.0,
                                     in1=all_tiles("a_exp"), op0=ALU.mult, op1=ALU.mult).then_inc(decay_ready, 1)
            dve.wait_ge(decay_exps, 1)
            dve.tensor_tensor(cols("beta_exp"), cols("beta"), cols("cum_exp"), ALU.mult).then_inc(beta_exp_ready, 1)
            for i in range(4):
                take_root(f"swa_q{i}")
                dve.scalar_tensor_tensor(out=Y[:, i, :], in0=Y[:, i, :], scalar=vec("swa_q"), in1=ps[:, ROOT, :],
                                         op0=ALU.mult, op1=ALU.mult).then_inc(root_read, 1)
            for i in range(2):
                take_root(f"swa_k{i}")
                up, down = Y[:, 4 + 2 * i, :], Y[:, 5 + 2 * i, :]
                step(dve.memset(down[0:SW_D, :], 0.0))
                step(dve.scalar_tensor_tensor(out=down[SW_D:P, :], in0=up[SW_D:P, :], scalar=vec("swa_k")[SW_D:P, :],
                                              in1=ps[SW_D:P, ROOT, :], op0=ALU.mult, op1=ALU.mult))
                step(dve.scalar_tensor_tensor(out=up[0:SW_D, :], in0=up[0:SW_D, :], scalar=vec("swa_k")[0:SW_D, :],
                                              in1=ps[0:SW_D, ROOT, :], op0=ALU.mult, op1=ALU.mult))
                dve.memset(up[SW_D:P, :], 0.0).then_inc(root_read, 1)
            dve.wait_ge(bias_loaded, 16 * SW_H)
            attend(32, lambda n: P if n % 4 == 0 else 2 * P, 8, "swa")

            dve.memset(raw4[:, :, 0:DN_TAPS - 1], 0.0).then_inc(pads_zeroed, 1)
            dve.wait_ge(pads_zeroed, 2)
            for m in range(6):
                emptied(dve, START["qkv"] + m)
                for k in range(DN_TAPS):
                    for n in range(2):
                        t = 2 * m + n
                        w, src = vec("dn_conv", 12 * k + t), raw4[:, 2 * (m % 2) + n, k:k + SEQ]
                        if k:
                            dve.wait_ge(dn_taps_done, 6 * m + 2 * (k - 1) + n + 1)
                            ins = dve.scalar_tensor_tensor(out=Z[:, t, :], in0=src, scalar=w, in1=Z[:, t, :],
                                                           op0=ALU.mult, op1=ALU.add)
                        else:
                            ins = dve.tensor_scalar(Z[:, t, :], src, w, None, ALU.mult)
                        ins.then_inc(dn_conv_ready if k == DN_TAPS - 1 else dn_taps_done, 1)
            for i in range(8):
                take_root(f"dn_in{i}")
                dve.tensor_tensor(Z[:, i, :], Z[:, i, :], ps[:, ROOT, :], ALU.mult).then_inc(root_read, 1)

            dve.wait_ge(root_read, READS0["dn_in7"] + 1)
            step(dve.memset(Y[:, 4, :], 0.0))
            ident_h = bcast_heads(ident)
            for t in range(TT):
                tok = slice(t * P, (t + 1) * P)
                k0 = COLS["decay"][0] + DN_H * t
                dve.tensor_copy(by_head(E[:, 0, :]), small[:, k0:k0 + DN_H].unsqueeze(2)
                                .to_broadcast([P, DN_H, P])).then_inc(spread_ready, 1)
                dve.wait_ge(row_exp_ready, t + 1)
                for h in range(DN_H):
                    hp = slice(h * P, (h + 1) * P)
                    dve.scalar_tensor_tensor(out=E[:, 2, hp], in0=ps[:, 4, hp], scalar=col("cum", DN_H * t + h),
                                             in1=const("decay_mask"), op0=ALU.subtract, op1=ALU.add)
                    ins = dve.scalar_tensor_tensor(out=E[:, 3, hp], in0=ps[:, 4, hp],
                                                   scalar=col("cum", DN_H * t + h), in1=const("decay_mask_t"),
                                                   op0=ALU.subtract, op1=ALU.add)
                ins.then_inc(diffs_ready, 1)
                dve.scalar_tensor_tensor(out=by_head(Y[:, 3, :]), in0=Z[:, 0:DN_H, tok], scalar=float(P) ** -0.5,
                                         in1=by_head(E[:, 1, :]), op0=ALU.mult, op1=ALU.mult).then_inc(qe_ready, 1)
                dve.wait_ge(decays_ready, t + 1)
                dve.wait_ge(products_ready, t + 1)
                for h in range(DN_H):
                    hp = slice(h * P, (h + 1) * P)
                    ins = dve.scalar_tensor_tensor(out=E[:, 2, hp], in0=ps[:, 5, hp], scalar=col("beta", DN_H * t + h),
                                                   in1=E[:, 2, hp], op0=ALU.mult, op1=ALU.mult)
                ins.then_inc(a_ready, 1)
                dve.scalar_tensor_tensor(out=E[:, 3, :], in0=ps[:, 6, :], scalar=float(P) ** -0.5, in1=E[:, 3, :],
                                         op0=ALU.mult, op1=ALU.mult).then_inc(qk_ready, 1)
                dve.wait_ge(a_ready, t + 1)
                for lv in range(6):
                    mask = bcast_heads(const("inv_mask")[:, lv * P:(lv + 1) * P])
                    if lv:
                        dve.wait_ge(level_p, 5 * t + lv)
                        src = by_head(ps[:, 1, :])
                    else:
                        src = by_head(E[:, 2, :])
                    dve.tensor_tensor(by_head(Y[:, 5, :]), src, mask, ALU.mult).then_inc(level_m, 1)
                    if lv == 0:
                        dve.wait_ge(level_m, 6 * t + 1)
                        dve.tensor_tensor(by_head(Y[:, 6, :]), ident_h, by_head(Y[:, 5, :]), ALU.subtract)
                    dve.wait_ge(level_qr, 6 * t + lv + 1)
                    if lv == 0:
                        dve.tensor_tensor(by_head(Y[:, 7, :]), ident_h, by_head(ps[:, 3, :]),
                                          ALU.subtract).then_inc(level_t, 1)
                    else:
                        if lv < 5:
                            dve.tensor_tensor(Y[:, 6, :], Y[:, 6, :], ps[:, 2, :], ALU.subtract)
                        dve.tensor_tensor(Y[:, 7, :], Y[:, 7, :], ps[:, 3, :], ALU.subtract).then_inc(level_t, 1)
                    dve.wait_ge(level_t, 6 * t + lv + 1)
                dve.wait_ge(wu_copied, t + 1)
                for cc in range(2):
                    n = 2 * t + cc
                    r = slice(cc * DN_CH, (cc + 1) * DN_CH)
                    dve.wait_ge(ws_ready, n + 1)
                    dve.tensor_tensor(Y[r, 6, :], Y[r, 5, :], ps[r, 4, :], ALU.subtract).then_inc(new_ready, 1)
                    dve.wait_ge(o_ready, n + 1)
                    for h in range(DN_H):
                        hp = slice(h * P, (h + 1) * P)
                        last = h * P + cc * DN_CH + DN_CH - 1
                        ins = dve.scalar_tensor_tensor(out=Y[:, 4, hp], in0=Y[:, 4, hp],
                                                       scalar=E[:, 1, last:last + 1], in1=ps[:, 6, hp],
                                                       op0=ALU.mult, op1=ALU.add)
                    ins.then_inc(state_ready, 1)
                    dve.wait_ge(state_ready, n + 1)
            base = SPLIT0["dn"]
            for i in range(DN_H):
                take_root(f"dn_out{i}")
                dve.scalar_tensor_tensor(out=Z[:, i, :], in0=Z[:, i, :], scalar=vec("dn_out"), in1=ps[:, ROOT, :],
                                         op0=ALU.mult, op1=ALU.mult).then_inc(root_read, 1)
                dve.wait_ge(root_read, READS0[f"dn_out{i}"] + 1)
                dve.wait_ge(split_done, base + i - 1)
                dve.tensor_tensor(NT[:, (base + i) % 2, :], Z[:, i, :], Z[:, 12 + i, :],
                                  ALU.mult).then_inc(gated_ready, 1)
                dve.wait_ge(split_hi, base + i + 1)
                dve.tensor_tensor(hl[:, i, :], NT[:, (base + i) % 2, :], hh[:, i, :],
                                  ALU.subtract).then_inc(split_done, 1)
            for m in range(4):
                c = START["merge"] + 4 * m
                y, term = Y[:, 2 * m:2 * m + 2, :], Z[:, 8:10, :]
                emptied(dve, c)
                emptied(dve, c + 1)
                multiplied(dve, c + 2)
                dve.tensor_tensor(y, ps[:, pair(c + 2):pair(c + 2) + 2, :], Z[:, 4:8:2, :],
                                  ALU.mult).then_inc(pair_free[c % 2], 1)
                multiplied(dve, c + 3)
                if m:
                    dve.wait_ge(merged_ready, m)
                dve.tensor_tensor(term, ps[:, pair(c + 3):pair(c + 3) + 2, :], Z[:, 5:8:2, :],
                                  ALU.mult).then_inc(pair_free[(c + 1) % 2], 1)
                emptied(dve, c + 2)
                emptied(dve, c + 3)
                dve.tensor_tensor(y, y, term, ALU.add).then_inc(merged_ready, 1)
            for j in range(DT):
                dve.wait_ge(split_hi, SPLIT0["merged"] + j + 1)
                dve.tensor_tensor(xl[:, j, :], Y[:, j, :], xh[:, j, :], ALU.subtract).then_inc(split_done, 1)

            def add_output(c, m, h=0):
                multiplied(dve, c, h)
                r = resid[:, 2 * m:2 * m + 2, :]
                dve.tensor_tensor(r, r, ps[:, pair(c):pair(c) + 2, :], ALU.add).then_inc(pair_free[c % 2], 1)

            for m in range(4):
                add_output(START["w_out"] + m, m)
            if upto == "merge": return
            for m in range(4):
                emptied(dve, START["w_out"] + m)
            norm_split("ffn2_pre", lambda j: resid[:, j, :], lambda j: vec("ffn_norm", j),
                       lambda j: xh[:, j, :], lambda j: xl[:, j, :])

            def gated_block(c0, n, b=0, base=0):
                for j in range(n):
                    c = c0 + j
                    p = c % 2
                    dve.wait_ge(gate_ready, b * 8 + (8 + base + j + 1))
                    dve.tensor_tensor(Z[:, 2 + p, :], ps[:, 2 * p + 1, :], Z[:, p, :],
                                      ALU.mult).then_inc(pair_free[p], 1)
                    dve.wait_ge(hidden_hi, b * 8 + (32 + base + j + 1))
                    dve.tensor_tensor(hl[:, j, :], Z[:, 2 + p, :], hh[:, j, :], ALU.subtract).then_inc(hidden_ready, 1)
                for m in range(4):
                    c = c0 + n + m
                    multiplied(dve, c, b * 6)
                    r = resid[:, 2 * m:2 * m + 2, :]
                    dve.tensor_tensor(r, r, ps[:, pair(c):pair(c) + 2, :], ALU.add).then_inc(pair_free[c % 2], 1)

            dve.wait_ge(split_done, SPLIT0["ffn2_pre"] + DT)
            with dve.Fori(0, 2) as b:
                gated_block(START["ffn_2"], 8, b)
            gated_block(START["ffn_2"] + 24, FF2_TILES[2], 0, 16)

        @block.tensor
        def _(pe):
            def stats(stage, weights=ones):
                n, base = SQUARES[stage], SQUARES0[stage]
                if STAGE_NO[stage]:
                    pe.wait_ge(root_ready, STAGE_NO[stage])
                for j in range(n):
                    pe.wait_ge(squares_ready, base + j + 1)
                    pe.matmul(ps[:, SUMS, :], weights, SQ[:, (base + j) % 2, :], start=j == 0,
                              stop=j == n - 1).then_inc(squares_summed, 1)

            def start_chunk(c, h=0):
                pe.wait_ge(lo_ready, h * 2 + (c + 1))
                if c >= 2:
                    pe.wait_ge(pair_free[c % 2], h + c // 2)

            def passes(hi, lo, whi_, wlo_):
                return ((whi_, hi), (whi_, lo), (wlo_, hi))

            def project(c, hi, lo, h=0, k_tiles=DT, k0=0, need=None, second=None):
                start_chunk(c, h)
                p = c % 2
                for n in range(2):
                    if n and second:
                        hi, lo = second
                    for k in range(k_tiles):
                        if need and n == 0:
                            need(k)
                        w = slice(k * 2 * P + n * P, k * 2 * P + (n + 1) * P)
                        for q, (wt, xt) in enumerate(passes(hi, lo, whi, wlo)):
                            ins = pe.matmul(ps[:, 2 * p + n, :], wt[:, p, w], xt[:, k0 + k, :],
                                            start=k == 0 and q == 0, stop=k == k_tiles - 1 and q == 2)
                ins.then_inc(chunk_done, 1)

            def operand(name):
                return lambda k: pe.wait_ge(split_done, SPLIT0[name] + k + 1)

            def project_tokens(c, k_tiles, n_out, need=None):
                start_chunk(c)
                p = c % 2
                per_bank = min(TT, SEQ // n_out)
                for t in range(TT):
                    dst = ps[:, 2 * p + t // per_bank, (t % per_bank) * n_out:(t % per_bank + 1) * n_out]
                    for k in range(k_tiles):
                        if need and t == 0:
                            need(k)
                        for q, (xt, wt) in enumerate(((xh, whi), (xh, wlo), (xl, whi))):
                            ins = pe.matmul(dst, xt[:, k, t * P:(t + 1) * P], wt[:, p, k * n_out:(k + 1) * n_out],
                                            start=k == 0 and q == 0, stop=k == k_tiles - 1 and q == 2)
                ins.then_inc(chunk_done, 1)

            pe.wait_ge(consts_loaded, 32)
            pe.wait_ge(rel_spread, 2)
            for h in range(SW_H):
                if h >= 2:
                    pe.wait_ge(rel_copied, h - 1)
                pe.matmul(ps[:, 6 + h % 2, 0:RELW], rel_wide[:, h, :], onehot, start=True,
                          stop=True).then_inc(rel_summed, 1)
            stats("mix0_pre")
            c0 = START["pw1"]
            project(c0, xh, xl, need=operand("mix0_pre"))
            project(c0 + 1, xh, xl)
            with pe.Fori(0, 3) as h:
                project(c0 + 2, xh, xl, h)
                project(c0 + 3, xh, xl, h)
            pe.wait_ge(root_ready, 1)
            for j in range(DT):
                pe.wait_ge(conv_ready, j + 1)
                ins = pe.matmul(ps[:, SUMS, :], ones, Y[:, j, :], start=j == 0, stop=j == DT - 1)
            ins.then_inc(mean_summed, 1)
            stats("ln")
            c0 = START["pw2"]
            for c in range(c0, c0 + 4):
                project(c, hh, hl, need=operand("ln") if c == c0 else None)

            def ffn(layer, name):
                c0 = START[f"ffn_{layer}"]
                pe.wait_ge(split_done, SPLIT0[name] + 1)
                with pe.Fori(0, FF_BLOCKS) as b:
                    for j in range(4):
                        project(c0 + j, xh, xl, b * 4, need=operand(name) if j == 0 else None)
                    for j in range(4, 8):
                        project(c0 + j, hh, hl, b * 4, need=(lambda k: pe.wait_ge(
                            hidden_ready, b * 4 + (16 * layer + k // 2 + 1)) if k % 2 == 0 else None)
                            if j == 4 else None)

            stats("mix0_post")
            stats("ffn0_pre")
            ffn(0, "ffn0_pre")
            stats("ffn0_post")
            if upto == "ffn0": return

            stats("mla_in")
            c = START["latent"]
            project(c, xh, xl, need=operand("mla_kv_in"))
            pe.wait_ge(split_done, SPLIT0["mla_q_in"] + DT)
            project(c + 1, xh, xl, second=(hh, hl))
            project(c + 2, hh, hl)
            emptied(pe, c + 1)
            pe.wait_ge(tables_loaded, 16)
            pe.matmul(ps[:, 6, :], rotate, E[:, 2, :], start=True, stop=True).then_inc(rotated, 1)
            stats("kv")
            stats("q")
            for m in range(4):
                project(START["uk"] + m, xh, xl, k_tiles=2, need=operand("kv") if m == 0 else None)
            for m in range(6):
                project(START["uq"] + m, xh, xl, k_tiles=3, k0=2, need=operand("q") if m == 0 else None)
            for r in range(4):
                if r == 0:
                    emptied(pe, START["uq"] + 4)
                if r == 2:
                    emptied(pe, START["uq"] + 5)
                if r >= 1:
                    pe.wait_ge(roped, r)
                pe.matmul(ps[:, 6 + (r + 1) % 2, :], rotate, SQ[:, r, :] if r < 2 else rope_raw[:, r - 2, :],
                          start=True, stop=True).then_inc(rotated, 1)
            for m in range(4):
                project_tokens(START["uv"] + m, 2, 256)
            for m in range(2):
                emptied(pe, START["wo"] - 1 - m)
            pe.wait_ge(roped, 5)
            pe.wait_ge(root_ready, STAGE_NO["q"] + 1)
            pe.wait_ge(root_read, READS0["q"] + 3)

            def attend(it0, n_keys, group, name, score, values):
                def scores(it):
                    if it - it0 >= 4:
                        pe.wait_ge(probs_scaled, it - 3)
                    score(it - it0, ps[:, SCORE[it % 4], :]).then_inc(scores_ready, 1)

                def turn(it):
                    pe.wait_ge(probs_scaled, it + 1)
                    if it >= 2:
                        pe.wait_ge(probs_back, it - 1)
                    for j in range(n_keys(it - it0) // P):
                        ins = pe.transpose(ps[:, TURN[it % 2], j * P:(j + 1) * P], NT[:, it % 2, j * P:(j + 1) * P],
                                           ident)
                    ins.then_inc(probs_turned, 1)

                def times_values(it):
                    blocks = n_keys(it - it0) // P
                    pe.wait_ge(probs_back, it + 1)
                    g = (it - it0) // group
                    if (it - it0) % group == 0 and g >= 2:
                        pe.wait_ge(split_done, SPLIT0[name] + g - 1)
                    dst, lhs = values(it - it0, ps[:, OUTPUT[g % 2], :])
                    for j in range(blocks):
                        ins = pe.matmul(dst, lhs(j), SQ[:, it % 2, j * P:(j + 1) * P], start=j == 0,
                                        stop=j == blocks - 1)
                    ins.then_inc(pv_done, 1)

                for it in range(it0, it0 + 3):
                    scores(it)
                for it in range(it0, it0 + 32):
                    if it + 3 < it0 + 32:
                        scores(it + 3)
                    turn(it)
                    if it > it0:
                        times_values(it - 1)
                times_values(it0 + 31)

            def mla_score(n, bank):
                h, i = n // 4, n % 4
                q, nk = slice(i * P, (i + 1) * P), (i + 1) * P
                pe.matmul(bank[:, 0:nk], Y[:, h, q], Z[:, h, 0:nk], start=True, stop=False)
                return pe.matmul(bank[:, 0:nk], E[:, h // 2, q], E[:, 4 + h % 2, 0:nk], start=False, stop=True)

            attend(0, lambda n: (n % 4 + 1) * P, 4, "heads", mla_score,
                   lambda n, bank: (bank[:, (n % 4) * P:(n % 4 + 1) * P],
                                    lambda j: V[:, j, (n // 4) * P:(n // 4 + 1) * P]))
            for m in range(4):
                project(START["wo"] + m, hh, hl, need=operand("heads") if m == 0 else None)
            stats("mix1_post")
            if upto == "mix1": return
            stats("ffn1_pre")
            ffn(1, "ffn1_pre")
            stats("ffn1_post")
            if upto == "ffn1": return

            stats("attn2")
            project_tokens(START["ba"], DT, 8, need=operand("attn2"))
            for m in range(2):
                project(START["sq"] + m, xh, xl)
            project(START["sk"], xh, xl)
            project_tokens(START["sv"], DT, P)
            pe.wait_ge(decay_ready, 1)
            pe.matmul(ps[:, 6, 0:16], const("tri"), cols("decay"), start=True, stop=True)
            pe.matmul(ps[:, 6, 16:32], const("rev"), cols("decay"), start=True, stop=True).then_inc(decay_summed, 1)
            for i in range(4):
                stats(f"swa_q{i}", half_ones)
            for i in range(2):
                stats(f"swa_k{i}", half_ones)
            emptied(pe, START["sv"])
            emptied(pe, START["sk"])
            pe.wait_ge(decay_exps, 1)
            pe.wait_ge(root_read, READS0["swa_k1"] + 1)

            def swa_score(n, bank):
                h, i = n // 4, n % 4
                nk = P if i == 0 else 2 * P
                keys = slice(max(i - 1, 0) * P, (i + 1) * P)
                return pe.matmul(bank[:, 0:nk], Y[:, h // 2, i * P:(i + 1) * P],
                                 Y[:, 4 + 2 * (h // 4) + h % 2, keys], start=True, stop=True)

            def swa_values(n, bank):
                h, i = n // 4, n % 4
                r = slice((h % 2) * SW_D, (h % 2 + 1) * SW_D)
                b0 = max(i - 1, 0)
                return (bank[r, i * P:(i + 1) * P],
                        lambda j: sv_tok[:, (b0 + j) * P + (h // 4) * SW_D:(b0 + j) * P + (h // 4 + 1) * SW_D])

            attend(32, lambda n: P if n % 4 == 0 else 2 * P, 8, "swa", swa_score, swa_values)
            pe.wait_ge(split_done, SPLIT0["swa"] + 4)

            for m in range(6):
                project(START["qkv"] + m, xh, xl)
            for m in range(2):
                project(START["z"] + m, xh, xl)
            for i in range(8):
                stats(f"dn_in{i}")
            pe.wait_ge(root_read, READS0["dn_in7"] + 1)
            for k in range(2):
                emptied(pe, START["merge"] - 1 - k)
            for t in range(TT):
                tok = slice(t * P, (t + 1) * P)
                heads = [(h, slice(h * P, (h + 1) * P)) for h in range(DN_H)]
                pe.wait_ge(spread_ready, t + 1)
                if t:
                    pe.wait_ge(state_ready, 2 * t)
                    pe.wait_ge(o_copied, 2 * t)
                for h, hp in heads:
                    ins = pe.matmul(ps[:, 4, hp], E[:, 0, hp], const("tri"), start=True, stop=True)
                ins.then_inc(rows_summed, 1)
                for h, hp in heads:
                    pe.matmul(ps[:, 5, hp], Z[:, DN_H + h, tok], Z[:, DN_H + h, tok], start=True, stop=True)
                for h, hp in heads:
                    ins = pe.matmul(ps[:, 6, hp], Z[:, DN_H + h, tok], Z[:, h, tok], start=True, stop=True)
                ins.then_inc(products_ready, 1)
                for h, hp in heads:
                    pe.transpose(ps[:, 7, hp], Z[:, DN_H + h, tok], ident)
                for h, hp in heads:
                    ins = pe.transpose(ps[:, 0, hp], Z[:, 2 * DN_H + h, tok], ident)
                ins.then_inc(tokens_turned, 1)
                pe.wait_ge(a_ready, t + 1)
                for h, hp in heads:
                    ins = pe.transpose(ps[:, 1, hp], E[:, 2, hp], ident)
                ins.then_inc(a_turned, 1)
                pe.wait_ge(at_ready, t + 1)
                for lv in range(6):
                    if lv:
                        pe.wait_ge(level_t, 6 * t + lv)
                        for h, hp in heads:
                            ins = pe.matmul(ps[:, 1, hp], Y[:, 1, hp], Y[:, 6, hp], start=True, stop=True)
                        ins.then_inc(level_p, 1)
                    pe.wait_ge(level_m, 6 * t + lv + 1)
                    if 0 < lv < 5:
                        for h, hp in heads:
                            pe.matmul(ps[:, 2, hp], Y[:, 7, hp], Y[:, 5, hp], start=True, stop=True)
                    for h, hp in heads:
                        ins = pe.matmul(ps[:, 3, hp], Y[:, 5, hp], Y[:, 7, hp] if lv else ident, start=True, stop=True)
                    ins.then_inc(level_qr, 1)
                pe.wait_ge(level_t, 6 * t + 6)
                pe.wait_ge(tok_ready, t + 1)
                for h, hp in heads:
                    pe.matmul(ps[:, 1, hp], E[:, 4, hp], Y[:, 7, hp], start=True, stop=True)
                for h, hp in heads:
                    ins = pe.matmul(ps[:, 2, hp], Y[:, 7, hp], E[:, 5, hp], start=True, stop=True)
                ins.then_inc(wu_ready, 1)
                pe.wait_ge(wu_copied, t + 1)
                pe.wait_ge(qe_ready, t + 1)
                pe.wait_ge(qk_ready, t + 1)
                for cc in range(2):
                    n = 2 * t + cc
                    r = slice(cc * DN_CH, (cc + 1) * DN_CH)
                    if n:
                        pe.wait_ge(state_ready, n)
                        pe.wait_ge(o_copied, n)
                    for h, hp in heads:
                        ins = pe.matmul(ps[r, 4, hp], Y[:, 2, h * P + cc * DN_CH:h * P + (cc + 1) * DN_CH],
                                        Y[:, 4, hp], start=True, stop=True)
                    ins.then_inc(ws_ready, 1)
                    pe.wait_ge(new_ready, n + 1)
                    for h, hp in heads:
                        ins = pe.matmul(ps[:, 6, hp], Y[r, 0, hp], Y[r, 6, hp], start=True, stop=True)
                    for h, hp in heads:
                        cs = slice(h * P + cc * DN_CH, h * P + (cc + 1) * DN_CH)
                        dst = ps[:, 5, h * DN_CH:(h + 1) * DN_CH]
                        pe.matmul(dst, Y[:, 4, hp], Y[:, 3, cs], start=True, stop=False)
                        o = pe.matmul(dst, Y[r, 6, hp], E[r, 3, cs], start=False, stop=True)
                    o.then_inc(o_ready, 1)
            for i in range(DN_H):
                stats(f"dn_out{i}")

            for m in range(4):
                c = START["merge"] + 4 * m
                project(c, xh, xl)
                project(c + 1, xh, xl)
                project(c + 2, hh, hl, k_tiles=4, need=operand("dn") if m == 0 else None)
                project(c + 3, hh, hl, k_tiles=4, k0=4)
            for m in range(4):
                project(START["w_out"] + m, xh, xl, need=operand("merged") if m == 0 else None)
            if upto == "merge": return
            stats("ffn2_pre")
            pe.wait_ge(split_done, SPLIT0["ffn2_pre"] + 1)

            def gated_block(c0, n, b=0, base=0):
                for j in range(n):
                    project(c0 + j, xh, xl, b * 6, need=operand("ffn2_pre") if j == 0 and base == 0 else None)
                for m in range(4):
                    project(c0 + n + m, hh, hl, b * 6, k_tiles=n, need=(lambda k: pe.wait_ge(
                        hidden_ready, b * 8 + (32 + base + k + 1))) if m == 0 else None)

            with pe.Fori(0, 2) as b:
                gated_block(START["ffn_2"], 8, b)
            gated_block(START["ffn_2"] + 24, FF2_TILES[2], 0, 16)


def pack(inputs):
    import numpy as np
    a = {n: np.asarray(v) for n, v in inputs.items()}
    stream = np.zeros((N_CHUNK, P, CW), np.float32)

    def put(c, w):
        k, n = w.shape[0] // P, w.shape[1]
        stream[c, :, 0:k * n] = w.reshape(k, P, n).transpose(1, 0, 2).reshape(P, k * n)

    def beside(*parts):
        return np.concatenate(parts, axis=1)

    c = START["pw1"]
    w = a["conv_w_pw1"][0]
    for j in range(8):
        put(c + j, beside(w[:, j * P:(j + 1) * P], w[:, D + j * P:D + (j + 1) * P]))
    for name, w, n in (("pw2", a["conv_w_pw2"][0], 4), ("wo", a["mla_w_o"][0], 4), ("w_out", a["w_out_2"][0], 4),
                       ("uk", a["kv_w_uk"], 4), ("uv", a["kv_w_uv"], 4)):
        for j in range(n):
            put(START[name] + j, w[:, j * 256:(j + 1) * 256])
    for layer in range(2):
        c = START[f"ffn_{layer}"]
        w1, w2 = a["w_ff1"][layer], a["w_ff2"][layer]
        for b in range(FF_BLOCKS):
            for j in range(4):
                put(c + 8 * b + j, w1[:, b * D + j * 256:b * D + (j + 1) * 256])
                put(c + 8 * b + 4 + j, w2[b * D:(b + 1) * D, j * 256:(j + 1) * 256])
    c = START["latent"]
    kr, dq = a["kv_w_kr"], a["mla_w_dq"][0]
    put(c, a["kv_w_dkv"])
    put(c + 1, beside(kr, kr, dq[:, 0:P]))
    put(c + 2, dq[:, P:3 * P])
    c, w = START["uq"], a["mla_w_uq"][0].reshape(Q_LORA, NH, QKD)
    for m in range(4):
        put(c + m, w[:, 2 * m:2 * m + 2, 0:NOPE].reshape(Q_LORA, 256))
    for m in range(2):
        put(c + 4 + m, w[:, 4 * m:4 * m + 4, NOPE:QKD].reshape(Q_LORA, 256))
    w = a["w_in_2"][0]
    put(START["ba"], w[:, 2048:2056])
    for j in range(2):
        put(START["sq"] + j, w[:, 2056 + 256 * j:2312 + 256 * j])
        put(START["z"] + j, w[:, 1536 + 256 * j:1792 + 256 * j])
    k0, k1 = w[:, 2568:2632], w[:, 2632:2696]
    put(START["sk"], beside(k0, k0, k1, k1))
    put(START["sv"], w[:, 2696:2824])
    for j in range(6):
        put(START["qkv"] + j, w[:, 256 * j:256 * (j + 1)])
    for m in range(4):
        c = START["merge"] + 4 * m
        for i in range(2):
            g = 2824 + (2 * m + i) * P
            put(c + i, beside(w[:, g:g + P], w[:, g + D:g + D + P]))
        put(c + 2, a["w_branch_dn_2"][0][:, m * 256:(m + 1) * 256])
        put(c + 3, a["w_branch_swa_2"][0][:, m * 256:(m + 1) * 256])
    c, t0 = START["ffn_2"], 0
    for n in FF2_TILES:
        for t in range(t0, t0 + n):
            put(c, beside(a["w_gate_2"][0][:, t * P:(t + 1) * P], a["w_up_2"][0][:, t * P:(t + 1) * P]))
            c += 1
        for m in range(4):
            put(c, a["w_down_2"][0][t0 * P:(t0 + n) * P, m * 256:(m + 1) * 256])
            c += 1
        t0 += n

    vecs = np.zeros((P, N_VEC), np.float32)
    for name, v in (("mix_pre", "mix_pre_g"), ("mix_post", "mix_post_g"), ("ffn_pre", "ffn_pre_g"),
                    ("ffn_post", "ffn_post_g"), ("b_pw1", "conv_b_pw1"), ("b_dw", "conv_b_dw"),
                    ("ln_g", "conv_ln_g"), ("ln_b", "conv_ln_b"), ("b_pw2", "conv_b_pw2"),
                    ("q_norm", "mla_q_norm_g"), ("kv_in", "kv_in_g"), ("kv_norm", "kv_norm_g"),
                    ("attn_norm", "attn_norm_2"), ("dn_out", "dn_out_norm_2"), ("ffn_norm", "ffn_norm_2"),
                    ("w_dw", "conv_w_dw"), ("dn_conv", "dn_conv_2")):
        v = a[v].reshape(-1, P)
        vecs[:, VEC[name]:VEC[name] + v.shape[0]] = v.T
    for name, v in (("swa_q", "swa_q_norm_2"), ("swa_k", "swa_k_norm_2")):
        for i in range(2):
            vecs[i * SW_D:(i + 1) * SW_D, VEC[name]] = a[v][0]

    consts = np.zeros((P, N_CONST), np.float32)

    def const(name, m):
        consts[:, CONST_COLS[name][0]:CONST_COLS[name][1]] = m

    i, j = np.indices((P, P))
    same = i // DN_CH == j // DN_CH
    const("ident", i == j)
    const("ones", np.ones((P, P)))
    const("half_ones", i // SW_D == j // SW_D)
    levels = [(i // (2 * b) == j // (2 * b)) & (i // b % 2 == 1) & (j // b % 2 == 0) for b in (1, 2, 4, 8, 16, 32)]
    const("inv_mask", np.concatenate(levels, axis=1))
    const("decay_mask", np.where(same & (i > j), 0.0, BIG))
    const("decay_mask_t", np.where(same & (i <= j), 0.0, -BIG))
    const("tri", same & (i <= j))
    const("rev", same & (i > j))
    inv = (1.0 / (np.float32(ROPE_BASE) ** (np.arange(0, ROPE, 2, dtype=np.float32) / np.float32(ROPE)))).astype(np.float32)
    ang = (np.arange(SEQ, dtype=np.float32)[None, :] * inv[:, None]).astype(np.float32)
    tables = np.zeros((P, 3, SEQ), np.float32)
    half = ROPE // 2
    for r in range(P):
        q = r % ROPE
        tables[(r - q) + (q + half) % ROPE, 0, r] = -1.0 if q < half else 1.0
    tables[:, 1] = np.tile(np.cos(ang), (4, 1))
    tables[:, 2] = np.tile(np.sin(ang), (4, 1))
    dist = 2 * P - 1 - np.arange(RELW)
    near = np.maximum(dist, 1).astype(np.float32)
    exact = BUCKETS // 2
    far = exact + (np.log(near / np.float32(exact)) / np.float32(math.log(MAX_DIST / exact))
                   * np.float32(BUCKETS - exact)).astype(np.int32)
    bucket = np.where(dist < exact, np.maximum(dist, 0), np.minimum(far, BUCKETS - 1))
    inside = (dist >= 0) & (dist < P)
    onehot = np.zeros((BUCKETS + 1, RELW), np.float32)
    onehot[:BUCKETS] = (np.arange(BUCKETS)[:, None] == bucket[None, :]) & inside[None, :]
    onehot[BUCKETS] = np.where(inside, 0.0, -BIG)
    x = a["x"][0].T.reshape(DT, P, SEQ).transpose(1, 0, 2)
    return {"stream": stream, "vecs": vecs, "consts": consts, "x": np.ascontiguousarray(x),
            "tables": tables, "onehot": onehot, "rel_bias": a["rel_bias_2"], "a_log": a["dn_a_log_2"][0],
            "dt_bias": a["dn_dt_bias_2"][0], "sinks": a["swa_sinks_2"][0]}


def kernel(**inputs):
    import numpy as np
    import concourse.bacc as bacc
    from concourse.bass_utils import run_bass_kernel_spmd

    arrays = pack(inputs)
    nc = bacc.Bacc("TRN2", target_bir_lowering=False, num_devices=1)
    A = {n: nc.dram_tensor(n, v.shape, F32, kind="ExternalInput").ap() for n, v in arrays.items()}
    out = nc.dram_tensor("out", (P, DT, SEQ), F32, kind="ExternalOutput").ap()
    build(nc, A, out)
    got = run_bass_kernel_spmd(nc, [arrays], core_ids=[0]).results[0]["out"]
    return np.ascontiguousarray(got.transpose(2, 1, 0).reshape(1, SEQ, D))
```

```python
import math
from contextlib import ExitStack

import concourse.bass as bass
from concourse import mybir
from concourse.alu_op_type import AluOpType as ALU

F32 = mybir.dt.float32
F32R = mybir.dt.float32r
ACT = mybir.ActivationFunctionType
AX_X = mybir.AxisListType.X

P = 128
SEQ = 512
TT = SEQ // P
D = 1024
DT = D // P
D_FF = 4096
FF_BLOCKS = D_FF // D
TAPS = 31
PAD = TAPS - 1
PE_TAPS, POOL_TAPS = 4, 7
DVE_TAPS = TAPS - PE_TAPS - POOL_TAPS
LAST_TAPS = 8
NH, NOPE, ROPE, QKD = 8, 128, 64, 192
Q_LORA, KV_LORA = 384, 256
DN_H, DN_TAPS, DN_CH = 4, 4, 64
SW_H, SW_D = 8, 64
D_FF2 = 2816
FF2_TILES = (8, 8, 6)
CW = 2048
RMS_EPS, LN_EPS = 1e-6, 1e-5
BIG = 1e30
ROPE_BASE = 10000.0
BUCKETS, MAX_DIST = 32, 128
RELW = 3 * P

CONST_COLS = {}
_at = 0
for _name, _n in (("ident", P), ("ones", P), ("half_ones", P), ("inv_mask", 6 * P),
                  ("decay_mask", P), ("decay_mask_t", P), ("tri", P), ("rev", P)):
    CONST_COLS[_name] = (_at, _at + _n)
    _at += _n
N_CONST = _at

COLS = {}
_at = 2
for _name, _n in (("max", 8), ("neg_max", 8), ("row_sum", 8), ("inv_sum", 8), ("sink_exp", 8),
                  ("ba", 8 * TT), ("beta", DN_H * TT), ("dt_in", DN_H * TT), ("decay", DN_H * TT),
                  ("abs_in", DN_H * TT), ("soft", DN_H * TT), ("cum", DN_H * TT), ("cum_exp", DN_H * TT),
                  ("beta_exp", DN_H * TT), ("rev_exp", DN_H * TT), ("a_log", DN_H), ("dt_bias", DN_H),
                  ("sinks", SW_H), ("a_exp", DN_H), ("state_decay", 4 * DN_H), ("rel", SW_H)):
    COLS[_name] = (_at, _at + _n)
    _at += _n
N_COLS = _at

VEC = {}
_at = 0
for _name, _n in (("mix_pre", 16), ("mix_post", 16), ("ffn_pre", 16), ("ffn_post", 16), ("b_pw1", 16),
                  ("b_dw", 8), ("ln_g", 8), ("ln_b", 8), ("b_pw2", 8), ("q_norm", 3), ("kv_in", 8),
                  ("kv_norm", 2), ("attn_norm", 8), ("dn_out", 1), ("ffn_norm", 8), ("swa_q", 1),
                  ("swa_k", 1), ("w_dw", 8 * TAPS), ("dn_conv", 12 * DN_TAPS)):
    VEC[_name] = _at
    _at += _n
N_VEC = _at

START, WIDTH = {}, []
for _name, _w in (("pw1", [CW] * 8), ("pw2", [CW] * 4), ("ffn_0", [CW] * 32), ("latent", [CW] * 3),
                  ("uk", [512] * 4), ("uq", [768] * 6), ("uv", [512] * 4), ("wo", [CW] * 4),
                  ("ffn_1", [CW] * 32), ("sq", [CW] * 2), ("sk", [CW]), ("sv_ba", [DT * (P + 8)]),
                  ("z", [CW] * 2), ("qkv", [CW] * 6), ("merge", [CW, CW, 1024, 1024] * 4),
                  ("w_out", [CW] * 4), ("ffn_2", [CW] * 30 + [1536] * 4)):
    START[_name] = len(WIDTH)
    WIDTH += _w
N_CHUNK = len(WIDTH)

STAGES = ([("mix0_pre", 8, 8), ("ln", 8, 8), ("mix0_post", 8, 8), ("ffn0_pre", 8, 8), ("ffn0_post", 8, 8),
           ("mla_in", 8, 16), ("kv", 2, 2), ("q", 3, 3), ("mix1_post", 8, 8), ("ffn1_pre", 8, 8),
           ("ffn1_post", 8, 8), ("attn2", 8, 8)] + [(f"swa_q{i}", 1, 1) for i in range(4)]
          + [(f"swa_k{i}", 1, 1) for i in range(2)] + [(f"dn_in{i}", 1, 1) for i in range(8)]
          + [(f"dn_out{i}", 1, 1) for i in range(4)] + [("ffn2_pre", 8, 8)])
STAGE_NO, SQUARES0, READS0, SQUARES, STAT_BANKS, ROOTS_BEFORE, READS_BEFORE = {}, {}, {}, {}, {}, {}, {}
_a = _b = 0
_last = {}
for _i, (_name, _n, _r) in enumerate(STAGES):
    STAGE_NO[_name], SQUARES0[_name], READS0[_name], SQUARES[_name] = _i, _a, _b, _n
    _a += _n
    _b += _r
    _banks = (6, 7) if _n == 1 and _name[-1] in "1357" else (4, 5)
    STAT_BANKS[_name] = _banks
    ROOTS_BEFORE[_name], READS_BEFORE[_name] = _last.get(_banks, (0, 0))
    _last[_banks] = (_i + 1, _b)

SPLIT0 = {}
_a = 0
for _name, _n in (("mix0_pre", 8), ("ln", 8), ("ffn0_pre", 8), ("mla_kv_in", 8), ("mla_q_in", 8), ("kv", 2),
                  ("q", 3), ("heads", 8), ("ffn1_pre", 8), ("attn2", 8), ("swa", 4), ("dn", 4),
                  ("merged", 8), ("ffn2_pre", 8)):
    SPLIT0[_name] = _a
    _a += _n
RES = {n: DT // 2 * i for i, n in enumerate(("mix0", "ffn0", "mix1", "ffn1"))}


def runs(first, last, breaks=()):
    found, c = [], first
    while c < last:
        n = 1
        while c + n < last and WIDTH[c + n] == WIDTH[c] and c + n not in breaks:
            n += 1
        found.append((c, n))
        c += n
    return found


def build(nc, A, out):
    ctx = ExitStack()
    with ctx:
        def sb(name, shape, dt=F32):
            return ctx.enter_context(nc.sbuf_tensor(name, shape, dt))

        def sem(name):
            return ctx.enter_context(nc.semaphore(name))

        wraw = sb("wraw", [P, 2, CW])
        whi = sb("whi", [P, 2, CW], F32R)
        wlo = sb("wlo", [P, 2, CW], F32R)
        resid = sb("resid", [P, DT, SEQ])
        xh = sb("xh", [P, DT, SEQ], F32R)
        xl = sb("xl", [P, DT, SEQ], F32R)
        hh = sb("hh", [P, DT, SEQ], F32R)
        hl = sb("hl", [P, DT, SEQ], F32R)
        Y = sb("Y", [P, DT, SEQ])
        Z = sb("Z", [P, 16, SEQ])
        E = sb("E", [P, 6, SEQ])
        SQ = sb("SQ", [P, 2, SEQ])
        NT = sb("NT", [P, 2, SEQ])
        K = sb("K", [P, N_CONST])
        PV = sb("PV", [P, N_VEC])
        small = sb("small", [P, N_COLS])
        ps = ctx.enter_context(nc.psum_tensor("ps", [P, 8, SEQ], F32))
        SUMS, ROOT = 4, 5
        SCORE, TURN, OUTPUT = (4, 5, 0, 1), (6, 2), (7, 3)

        def const(name):
            a, b = CONST_COLS[name]
            return K[:, a:b]

        def cols(name):
            a, b = COLS[name]
            return small[:, a:b]

        def col(name, i):
            return small[:, COLS[name][0] + i:COLS[name][0] + i + 1]

        ident, ones, half_ones = map(const, ("ident", "ones", "half_ones"))

        def vec(name, i=0):
            return PV[:, VEC[name] + i:VEC[name] + i + 1]

        eps_rms, eps_ln = small[:, 0:1], small[:, 1:2]
        UW = SEQ + PAD
        U = Z[:, 0:9, :].rearrange("p a b -> p (a b)")[:, 0:DT * UW].rearrange("p (t n) -> p t n", n=UW)

        diag = [[Z[:, 9 + j, k * P:(k + 1) * P] for k in range(PE_TAPS)] for j in range(2)]
        last_diag = [Z[:, 11 + i // 4, i % 4 * P:(i % 4 + 1) * P] for i in range(LAST_TAPS)]
        pool_sum, TAP_BANK = (E[:, 0, :], E[:, 1, :]), (6, 7)
        product = [E[:, 2 + i % 4, :] for i in range(POOL_TAPS)]

        cos_t, sin_t, rotate = Z[:, 14, :], Z[:, 15, :], Z[:, 13, 0:P]
        V = Z[:, 8:16, :].rearrange("p (t a) n -> p t (a n)", t=TT)
        rope_raw = Z[:, 8:10, :]
        onehot = E[0:BUCKETS + 1, 0, 0:RELW]
        rel_wide = E[0:BUCKETS + 1, 1:3, :].rearrange("p a n -> p (a n)").rearrange("p (h n) -> p h n", n=P)
        rel_rows = [E[:, 3:6, :].rearrange("p a n -> p (a n)").rearrange("p (h n) -> p h n", n=RELW),
                    Z[:, 9:12, :].rearrange("p a n -> p (a n)").rearrange("p (h n) -> p h n", n=RELW)]
        bias = E[:, 0:4, :].rearrange("p a n -> p (a n)").rearrange("p (h n) -> p h n", n=2 * P)
        rel_scratch = nc.dram_tensor("rel_scratch", (SW_H, P, RELW), F32, kind="Internal")
        sv_tok = E[:, 4, :]
        RW = SEQ + DN_TAPS - 1
        raw4 = E[:, 0:5, :].rearrange("p a n -> p (a n)")[:, 0:4 * RW].rearrange("p (a n) -> p a n", n=RW)

        spread, row_exp, a_mat, a_turn = E[:, 0, :], E[:, 1, :], E[:, 2, :], Y[:, 5, :]
        level_mask = E[:, 0, :]
        qk, kbe_w = (E[:, 3, :], NT[:, 0, :]), (E[:, 4, :], NT[:, 1, :])
        vb_u, k_rev, q_exp = (E[:, 5, :], SQ[:, 0, :]), (Y[:, 0, :], SQ[:, 1, :]), (Y[:, 3, :], Y[:, 1, :])
        state, v_new = Y[:, 4, :], Y[:, 2, :]
        inverse = (Y[:, 6, :], Y[:, 7, :])
        HALF = SEQ // 2
        ROWS, KK, KQ, K_TOK, V_TOK, A_TURN, W_BANK, U_BANK = 7, 2, 3, 0, 1, 7, 0, 1
        LEVEL_P, LEVEL_QR = (0, 1), (2, 3)
        WS, OUT, STATE = 4, 5, 6

        def by_head(t):
            return t.rearrange("p (h n) -> p h n", n=P)

        def bcast_heads(m):
            return m.unsqueeze(1).to_broadcast([P, DN_H, P])

        raw_loaded = [sem("raw_loaded_even"), sem("raw_loaded_odd")]
        hi_ready, lo_ready, chunk_done = sem("hi_ready"), sem("lo_ready"), sem("chunk_done")
        pair_free = [sem("pair_free_even"), sem("pair_free_odd")]
        ones_loaded, vecs_loaded, onehot_loaded = sem("ones_loaded"), sem("vecs_loaded"), sem("onehot_loaded")
        consts_loaded, x_loaded = sem("consts_loaded"), [sem(f"x_loaded_{i}") for i in range(DT // 2)]
        eps_ready, pads_zeroed, y_zeroed = sem("eps_ready"), sem("pads_zeroed"), sem("y_zeroed")
        dve_step, act_step = sem("dve_step"), sem("act_step")
        resid_ready, resid_odd_ready = sem("resid_ready"), sem("resid_odd_ready")
        squares_ready, squares_summed = sem("squares_ready"), sem("squares_summed")
        root_ready, root_read = sem("root_ready"), sem("root_read")
        split_hi, split_done = sem("split_hi"), sem("split_done")
        gate_ready, taps_done, conv_ready = sem("gate_ready"), sem("taps_done"), sem("conv_ready")
        diag_ready, pe_taps_done, products_scaled, products_added = map(
            sem, ("diag_ready", "pe_taps_done", "products_scaled", "products_added"))
        mean_summed, centred = sem("mean_summed"), sem("centred")
        hidden_sq, hidden_hi, hidden_ready = map(sem, ("hidden_sq", "hidden_hi", "hidden_ready"))
        out_stored = sem("out_stored")
        tables_loaded, rows_loaded = sem("tables_loaded"), sem("rows_loaded")
        rel_summed, rel_copied, rel_stored, bias_loaded, rel_spread = map(
            sem, ("rel_summed", "rel_copied", "rel_stored", "bias_loaded", "rel_spread"))
        rotated, roped = sem("rotated"), sem("roped")
        scores_ready, max_ready, probs_ready, probs_scaled, probs_turned, probs_back, pv_done = map(
            sem, ("scores_ready", "max_ready", "probs_ready", "probs_scaled", "probs_turned", "probs_back",
                  "pv_done"))
        swa_keys_ready, swa_ready = sem("swa_keys_ready"), sem("swa_ready")
        ba_ready, softplus_in, softplus_out, decay_ready, decay_summed, decay_exps, beta_exp_ready = map(
            sem, ("ba_ready", "softplus_in", "softplus_out", "decay_ready", "decay_summed", "decay_exps",
                  "beta_exp_ready"))
        dn_taps_done, dn_conv_ready, dn_silu_ready = map(sem, ("dn_taps_done", "dn_conv_ready", "dn_silu_ready"))
        spread_ready, rows_summed, products_ready, tokens_turned = map(
            sem, ("spread_ready", "rows_summed", "products_ready", "tokens_turned"))
        row_exp_ready, diffs_ready, decays_ready, a_ready, qk_ready, qe_ready, tok_ready = map(
            sem, ("row_exp_ready", "diffs_ready", "decays_ready", "a_ready", "qk_ready", "qe_ready", "tok_ready"))
        a_turned, at_ready, level_p, level_m, level_qr, level_t, wu_ready, wu_copied = map(
            sem, ("a_turned", "at_ready", "level_p", "level_m", "level_qr", "level_t", "wu_ready", "wu_copied"))
        ws_ready, new_ready, o_ready, o_copied, state_ready = map(
            sem, ("ws_ready", "new_ready", "o_ready", "o_copied", "state_ready"))
        gated_ready, gates_ready, merged_ready, swa_term = map(
            sem, ("gated_ready", "gates_ready", "merged_ready", "swa_term"))

        block = ctx.enter_context(nc.Block())

        def tap(k, j, h=0):
            if isinstance(h, int):
                return vec("w_dw", k * DT + 2 * h + j)
            return PV[:, bass.ds(h * 2 + (VEC["w_dw"] + k * DT + j), 1)]

        def shifted(k, j, h=0):
            t = 2 * h + j if isinstance(h, int) else h * 2 + j
            return U[:, t, k:k + SEQ] if isinstance(h, int) else U[:, bass.ds(t, 1), k:k + SEQ]

        def gated(eng, j, h=0):
            eng.wait_ge(pair_free[j % 2], h + (j // 2 + 1))

        def pair(c):
            return 2 * (c % 2)

        _p = pair(START["sv_ba"])
        sv_ba = ps[:, _p:_p + 2, 0:2 * (P + 8)].rearrange("p b (t n) -> p b t n", t=2)

        def emptied(eng, c, h=0):
            eng.wait_ge(pair_free[c % 2], h + (c // 2 + 1))

        def multiplied(eng, c, h=0):
            eng.wait_ge(chunk_done, h * 2 + (c + 1))

        def resid_at(eng, name):
            return lambda j: eng.wait_ge(resid_odd_ready if j % 2 else resid_ready, RES[name] + j // 2 + 1)

        def resid_all(eng, name):
            for j in (DT - 2, DT - 1):
                resid_at(eng, name)(j)

        @block.sync
        def _(sp):
            def load(c, h=0):
                p, w = c % 2, WIDTH[c]
                if c >= 2:
                    sp.wait_ge(lo_ready, h * 2 + (c - 1))
                src = A["stream"][c, :, 0:w] if isinstance(h, int) else A["stream"][bass.ds(h * 2 + c, 1), :, 0:w]
                dst = wraw[:, p, 0:w]
                if not isinstance(h, int):
                    src = src.rearrange("a p n -> p (a n)")
                sp.dma_start(dst, src).then_inc(raw_loaded[p], 16)

            sp.dma_start(K[:, 0:2 * P], A["consts"][:, 0:2 * P]).then_inc(ones_loaded, 16)
            for j in range(0, DT, 2):
                sp.dma_start(resid[:, j:j + 2, :], A["x"][:, j:j + 2, :]).then_inc(x_loaded[j // 2], 16)
            sp.dma_start(PV[:, :], A["vecs"]).then_inc(vecs_loaded, 16)
            load(0)
            load(1)
            sp.dma_start(K[:, 2 * P:N_CONST], A["consts"][:, 2 * P:N_CONST]).then_inc(consts_loaded, 16)
            sp.dma_start(small[0:BUCKETS, COLS["rel"][0]:COLS["rel"][1]], A["rel_bias"]).then_inc(rows_loaded, 16)
            for n in ("a_log", "dt_bias", "sinks"):
                sp.dma_start(cols(n), A[n].partition_broadcast(P)).then_inc(rows_loaded, 16)
            sp.dma_start(Z[:, 13:16, :], A["tables"]).then_inc(tables_loaded, 16)
            for c, n in runs(2, N_CHUNK, (START["pw2"] + 2, START["ffn_0"] + 4, START["sq"] + 2)):
                if c == START["pw2"] + 2:
                    sp.wait_ge(conv_ready, DT)
                    sp.dma_start(onehot, A["onehot"]).then_inc(onehot_loaded, 16)
                if c == START["ffn_0"] + 4:
                    for g in range(2):
                        sp.wait_ge(rel_copied, 4 * (g + 1))
                        sp.dma_start(rel_scratch.ap()[4 * g:4 * g + 4].rearrange("h p n -> p h n"),
                                     rel_rows[g]).then_inc(rel_stored, 16)
                if c == START["sq"] + 2:
                    sp.wait_ge(rel_stored, 32)
                    resid_all(sp, "mix1")
                    for h in range(SW_H):
                        src = bass.AP(rel_scratch, h * P * RELW + P - 1, [[RELW - 1, P], [1, 2 * P]])
                        sp.dma_start(bias[:, h, :], src).then_inc(bias_loaded, 16)
                if n > 3:
                    with sp.Fori(0, n // 2) as h:
                        load(c, h)
                        load(c + 1, h)
                    if n % 2:
                        load(c + n - 1)
                else:
                    for k in range(n):
                        load(c + k)
            for m in range(4):
                emptied(sp, N_CHUNK - 4 + m)
                sp.dma_start(out[:, 2 * m:2 * m + 2, :], resid[:, 2 * m:2 * m + 2, :]).then_inc(out_stored, 16)
            sp.wait_ge(out_stored, 64)

        @block.gpsimd
        def _(pool):
            def rest(c, h=0):
                p, w = c % 2, WIDTH[c]
                pool.wait_ge(hi_ready, h * 2 + (c + 1))
                if c >= 2:
                    pool.wait_ge(chunk_done, h * 2 + (c - 1))
                pool.tensor_tensor(wlo[:, p, 0:w], wraw[:, p, 0:w], whi[:, p, 0:w],
                                   ALU.subtract).then_inc(lo_ready, 1)

            rest(0)
            rest(1)
            with pool.Fori(0, DT // 2) as h:
                for j in range(2):
                    rest(2 + j, h)
                    for i in range(1, POOL_TAPS):
                        pool.wait_ge(products_scaled, h * (2 * POOL_TAPS) + (j * POOL_TAPS + i + 1))
                        if i > 1:
                            pool.wait_ge(products_added, h * (2 * POOL_TAPS - 2) + (j * (POOL_TAPS - 1) + i - 1))
                        pool.tensor_tensor(pool_sum[j], product[0] if i == 1 else pool_sum[j], product[i],
                                           ALU.add).then_inc(products_added, 1)
            adds = {START["ffn_0"] + 1: "mix0_post", START["latent"] + 1: "ffn0_post",
                    START["ffn_1"] + 1: "mix1_post", START["sq"] + 1: "ffn1_post"}
            for c, n in runs(DT + 2, N_CHUNK, adds):
                if c in adds:
                    for j in range(1, DT, 2):
                        pool.wait_ge(root_read, READS0[adds[c]] + j + 1)
                        pool.tensor_tensor(resid[:, j, :], resid[:, j, :], Y[:, j, :],
                                           ALU.add).then_inc(resid_odd_ready, 1)
                if n > 3:
                    with pool.Fori(0, n // 2) as h:
                        rest(c, h)
                        rest(c + 1, h)
                    if n % 2:
                        rest(c + n - 1)
                else:
                    for k in range(n):
                        rest(c + k)

        @block.scalar
        def _(act):
            steps = [0]

            def step(ins):
                steps[0] += 1
                ins.then_inc(act_step, 1)
                act.wait_ge(act_step, steps[0])

            def head(c, h=0):
                if isinstance(h, int) and c + 2 * h >= N_CHUNK:
                    return
                p = c % 2
                w = WIDTH[c + 2 * h] if isinstance(h, int) else CW
                act.wait_ge(raw_loaded[p], h * 16 + 16 * (c // 2 + 1))
                if c >= 2:
                    act.wait_ge(chunk_done, h * 2 + (c - 1))
                act.activation(whi[:, p, 0:w], wraw[:, p, 0:w], ACT.Copy).then_inc(hi_ready, 1)

            def square(stage, src, j=0):
                at = SQUARES0[stage] + j
                if at >= 2:
                    act.wait_ge(squares_summed, at - 1)
                act.activation(SQ[:, at % 2, :], src, ACT.Square).then_inc(squares_ready, 1)

            def root(stage, n_feat, eps):
                sums, rt = STAT_BANKS[stage]
                act.wait_ge(squares_summed, SQUARES0[stage] + SQUARES[stage])
                if READS_BEFORE[stage]:
                    act.wait_ge(root_read, READS_BEFORE[stage])
                step(act.activation(ps[:, rt, :], ps[:, sums, :], ACT.Ln, scale=1.0 / n_feat, bias=eps))
                act.activation(ps[:, rt, :], ps[:, rt, :], ACT.Exp, scale=-0.5).then_inc(root_ready, 1)

            def stats(stage, src, ready, n_feat, eps):
                for j in range(SQUARES[stage]):
                    ready(j)
                    square(stage, src(j), j)
                root(stage, n_feat, eps)

            def square_pair(stage, src, c, m):
                if m < 3:
                    head(c + 2)
                emptied(act, c)
                for j in (2 * m, 2 * m + 1):
                    square(stage, src[:, j, :], j)
                if m == 3:
                    head(c + 2)

            def split_heads(name, dst, n=8, read0=None):
                for j in range(n):
                    act.wait_ge(root_read, (READS0[name] if read0 is None else read0) + j + 1)
                    act.activation(dst(j), NT[:, (SPLIT0[name] + j) % 2, :], ACT.Copy).then_inc(split_hi, 1)

            def root_table():
                act.preload_act_table_set("natural_log_exp_and_others")

            root_table()
            act.wait_ge(eps_ready, 2)
            for j in range(DT):
                act.wait_ge(x_loaded[j // 2], 16)
                square("mix0_pre", resid[:, j, :], j)
            head(0)
            root("mix0_pre", D, eps_rms)
            split_heads("mix0_pre", lambda j: xh[:, j, :])
            head(1)

            act.wait_ge(vecs_loaded, 16)
            act.wait_ge(ones_loaded, 16)
            for i in range(LAST_TAPS):
                act.activation(last_diag[i], ident, ACT.Copy, scale=tap(PE_TAPS + POOL_TAPS + i, 1, DT // 2 - 1))
            c0 = START["pw1"]
            with act.Fori(0, 4) as h:
                for j in range(2):
                    multiplied(act, c0 + j, h)
                    act.activation(SQ[:, j, :], ps[:, 2 * j + 1, :], ACT.Sigmoid,
                                   bias=PV[:, bass.ds(h * 2 + (VEC["b_pw1"] + DT + j), 1)]).then_inc(gate_ready, 1)
                    head(c0 + j + 2, h)
                    for k in range(PE_TAPS):
                        ins = act.activation(diag[j][k], ident, ACT.Copy, scale=tap(k, j, h))
                    ins.then_inc(diag_ready, 1)
                    gated(act, j, h)
                    act.wait_ge(lo_ready, h * 2 + (j + 3))
                    for i in range(POOL_TAPS):
                        if i >= 4:
                            act.wait_ge(products_added, h * (2 * POOL_TAPS - 2) +
                                        (j * (POOL_TAPS - 1) + max(1, i - 4)))
                        act.activation(product[i].unsqueeze(1), shifted(PE_TAPS + i, j, h), ACT.Copy,
                                       scale=tap(PE_TAPS + i, j, h)).then_inc(products_scaled, 1)
            root_table()
            def conv_centred(j):
                act.wait_ge(centred, j + 1)
            stats("ln", lambda j: Y[:, j, :], conv_centred, D, eps_ln)
            base = SPLIT0["ln"]
            for j in range(DT):
                act.wait_ge(root_read, READS0["ln"] + j + 1)
                if j >= 2:
                    act.wait_ge(split_done, base + j - 1)
                step(act.activation(NT[:, (base + j) % 2, :], Y[:, j, :], ACT.Silu,
                                    scale=vec("ln_g", j), bias=vec("ln_b", j)))
                act.activation(hh[:, j, :], NT[:, (base + j) % 2, :], ACT.Copy).then_inc(split_hi, 1)
            root_table()
            c0 = START["pw2"]
            for c in range(c0, c0 + 4):
                multiplied(act, c)
                for n in range(2):
                    j = 2 * (c - c0) + n
                    ins = act.activation(Y[:, j, :], ps[:, pair(c) + n, :], ACT.Identity, bias=vec("b_pw2", j))
                ins.then_inc(pair_free[c % 2], 1)
                square_pair("mix0_post", Y, c, c - c0)
            root("mix0_post", D, eps_rms)

            def pre(stage, name):
                stats(stage, lambda j: resid[:, j, :], resid_at(act, name), D, eps_rms)

            def ffn(layer):
                c0 = START[f"ffn_{layer}"]

                def block_of(b, last=False):
                    for j in range(8):
                        c = c0 + j
                        p = c % 2
                        multiplied(act, c, b * 4)
                        if j < 4:
                            relu = Z[:, 2 * p:2 * p + 2, :]
                            act.activation(relu, ps[:, 2 * p:2 * p + 2, :], ACT.Relu).then_inc(pair_free[p], 1)
                            act.wait_ge(hidden_sq, b * 4 + (16 * layer + j + 1))
                            act.activation(hh[:, 2 * j:2 * j + 2, :], Z[:, 4 + 2 * p:6 + 2 * p, :],
                                           ACT.Copy).then_inc(hidden_hi, 1)
                        if not (last and j >= 4):
                            head(c + 2, b * 4)
                        else:
                            square_pair(f"ffn{layer}_post", Y, c + 8 * b, j - 4)

                with act.Fori(0, FF_BLOCKS - 1) as b:
                    block_of(b)
                block_of(FF_BLOCKS - 1, True)
                root(f"ffn{layer}_post", D, eps_rms)

            for h in range(SW_H):
                act.wait_ge(rel_summed, h + 1)
                act.activation(rel_rows[h // 4][:, h % 4, :], ps[:, 6 + h % 2, 0:RELW],
                               ACT.Copy).then_inc(rel_copied, 1)
            pre("ffn0_pre", "mix0")
            split_heads("ffn0_pre", lambda j: xh[:, j, :])
            ffn(0)

            def copy_pair(c, dst):
                multiplied(act, c)
                act.activation(dst, ps[:, pair(c):pair(c) + 2, :], ACT.Copy).then_inc(pair_free[c % 2], 1)

            pre("mla_in", "ffn0")
            split_heads("mla_kv_in", lambda j: xh[:, j, :], read0=READS0["mla_in"])
            split_heads("mla_q_in", lambda j: hh[:, j, :], read0=READS0["mla_in"] + DT)
            c0 = START["latent"]
            act.wait_ge(rel_stored, 32)
            for m in range(2):
                copy_pair(c0 + m, E[:, 2 * m:2 * m + 2, :])
                head(c0 + m + 2)
                if m == 0:
                    emptied(act, c0)
                    for j in range(2):
                        square("kv", E[:, j, :], j)
            root("kv", KV_LORA, eps_rms)
            split_heads("kv", lambda j: xh[:, j, :], 2)
            copy_pair(c0 + 2, E[:, 4:6, :])
            head(c0 + 4)
            emptied(act, c0 + 2)
            for m in range(4):
                if m == 0:
                    square("q", E[:, 3, :], 0)
                    square("q", E[:, 4, :], 1)
                if m == 2:
                    square("q", E[:, 5, :], 2)
                    root("q", Q_LORA, eps_rms)
                    split_heads("q", lambda j: xh[:, 2 + j, :], 3)
                copy_pair(START["uk"] + m, Z[:, 2 * m:2 * m + 2, :])
                head(START["uk"] + m + 2)
            for m in range(6):
                copy_pair(START["uq"] + m, Y[:, 2 * m:2 * m + 2, :] if m < 4 else
                          (SQ[:, :, :] if m == 4 else rope_raw))
                head(START["uq"] + m + 2)
            act.wait_ge(roped, 5)
            for m in range(4):
                c = START["uv"] + m
                multiplied(act, c)
                act.activation(V[:, :, m * 256:(m + 1) * 256],
                               ps[:, pair(c):pair(c) + 2, :].rearrange("p b (t n) -> p (b t) n", n=256),
                               ACT.Copy).then_inc(pair_free[c % 2], 1)
                head(c + 2)

            def attend(it0, n_keys, scale, group, split, dst):
                def back(it):
                    nk = n_keys(it - it0)
                    act.wait_ge(probs_turned, it + 1)
                    if it >= 2:
                        act.wait_ge(pv_done, it - 1)
                    act.activation(SQ[:, it % 2, 0:nk], ps[:, TURN[it % 2], 0:nk], ACT.Copy).then_inc(probs_back, 1)

                def output(g):
                    act.wait_ge(pv_done, it0 + group * (g + 1))
                    act.activation(dst(g), ps[:, OUTPUT[g % 2], :], ACT.Copy).then_inc(split_hi, 1)

                for it in range(it0, it0 + 32):
                    k, s = it % 8, ps[:, SCORE[it % 4], 0:n_keys(it - it0)]
                    act.wait_ge(max_ready, it + 1)
                    if it0:
                        act.activation(col("sink_exp", k), col("sinks", (it - it0) // 4), ACT.Exp,
                                       bias=col("neg_max", k))
                    act.activation(s, s, ACT.Exp, scale=scale, bias=col("neg_max", k),
                                   accum_out=col("row_sum", k)).then_inc(probs_ready, 1)
                    if it >= it0 + 2:
                        back(it - 2)
                    if it - it0 - 3 >= group and (it - it0 - 3) % group == 0:
                        output((it - it0 - 3) // group - 1)
                back(it0 + 30)
                back(it0 + 31)
                output(32 // group - 1)

            attend(0, lambda n: (n % 4 + 1) * P, QKD ** -0.5, 4, "heads", lambda g: hh[:, g, :])
            for m in range(4):
                copy_pair(START["wo"] + m, Y[:, 2 * m:2 * m + 2, :])
                square_pair("mix1_post", Y, START["wo"] + m, m)
            root("mix1_post", D, eps_rms)
            pre("ffn1_pre", "mix1")
            split_heads("ffn1_pre", lambda j: xh[:, j, :])
            ffn(1)

            pre("attn2", "ffn1")
            split_heads("attn2", lambda j: xh[:, j, :])
            for m in range(2):
                copy_pair(START["sq"] + m, Y[:, 2 * m:2 * m + 2, :])
                head(START["sq"] + m + 2)
            emptied(act, START["sq"] + 1)
            square("swa_q0", Y[:, 0, :])
            copy_pair(START["sk"], Y[:, 4:8:2, :])
            head(START["sk"] + 2)
            root("swa_q0", SW_D, eps_rms)
            square("swa_q1", Y[:, 1, :])
            c = START["sv_ba"]
            multiplied(act, c)
            act.activation(cols("ba").rearrange("p (b t n) -> p b t n", t=2, n=8), sv_ba[:, :, :, P:P + 8], ACT.Copy)
            act.activation(sv_tok.rearrange("p (b t n) -> p b t n", t=2, n=P), sv_ba[:, :, :, 0:P],
                           ACT.Copy).then_inc(pair_free[c % 2], 1)
            head(c + 2)
            emptied(act, c)
            act.wait_ge(rows_loaded, 64)
            ba = cols("ba").rearrange("p (t n) -> p t n", n=8)
            act.activation(cols("beta").rearrange("p (t n) -> p t n", n=DN_H), ba[:, :, 0:DN_H],
                           ACT.Sigmoid).then_inc(ba_ready, 1)
            root_table()
            act.wait_ge(softplus_in, 1)
            step(act.activation(cols("abs_in"), cols("dt_in"), ACT.Abs))
            step(act.activation(cols("soft"), cols("abs_in"), ACT.Exp, scale=-1.0))
            act.activation(cols("soft"), cols("soft"), ACT.Ln, bias=1.0).then_inc(softplus_out, 1)
            act.activation(cols("a_exp"), cols("a_log"), ACT.Exp).then_inc(softplus_out, 1)
            root("swa_q1", SW_D, eps_rms)
            for m in range(2):
                c = START["z"] + m
                square(f"swa_q{m + 2}", Y[:, m + 2, :])
                multiplied(act, c)
                act.activation(Z[:, 12 + 2 * m:14 + 2 * m, :], ps[:, pair(c):pair(c) + 2, :],
                               ACT.Silu).then_inc(pair_free[c % 2], 1)
                head(c + 2)
                root_table()
                if m:
                    square("swa_k0", Y[:, 4, :])
                root(f"swa_q{m + 2}", SW_D, eps_rms)
            square("swa_k1", Y[:, 6, :])
            for i in range(2):
                root(f"swa_k{i}", SW_D, eps_rms)
            act.wait_ge(root_read, READS0["swa_k1"] + 1)
            attend(32, lambda n: P if n % 4 == 0 else 2 * P, 1.0, 8, "swa", lambda g: hh[:, 4 + g, :])

            for m in range(6):
                c = START["qkv"] + m
                if m >= 2:
                    act.wait_ge(dn_conv_ready, 2 * (m - 1))
                else:
                    act.wait_ge(pads_zeroed, 2)
                copy_pair(c, raw4[:, 2 * (m % 2):2 * (m % 2) + 2, DN_TAPS - 1:RW])
                head(c + 2)
                if m == 0:
                    act.wait_ge(decay_summed, 1)
                    act.activation(cols("cum"), ps[:, 6, 0:16], ACT.Copy)
                    act.activation(cols("cum_exp"), ps[:, 6, 0:16], ACT.Exp)
                    act.activation(cols("rev_exp"), ps[:, 6, 16:32], ACT.Exp).then_inc(decay_exps, 1)
                if 1 <= m <= 4:
                    for i in (2 * m - 2, 2 * m - 1):
                        root(f"dn_in{i}", 1, eps_rms)
                act.wait_ge(dn_conv_ready, 2 * (m + 1))
                act.activation(Z[:, 2 * m:2 * m + 2, :], Z[:, 2 * m:2 * m + 2, :], ACT.Silu).then_inc(dn_silu_ready, 1)
                root_table()
                if m < 4:
                    act.wait_ge(dn_silu_ready, m + 1)
                    for i in (2 * m, 2 * m + 1):
                        square(f"dn_in{i}", Z[:, i, :])

            def copy_out(n):
                act.wait_ge(o_ready, n + 1)
                act.activation(Z[:, 0:DN_H, n * DN_CH:(n + 1) * DN_CH],
                               ps[:, OUT, 0:DN_H * DN_CH].rearrange("p (h n) -> p h n", n=DN_CH),
                               ACT.Copy).then_inc(o_copied, 1)

            for t in range(TT):
                par = t % 2
                act.wait_ge(rows_summed, t + 1)
                act.activation(row_exp, ps[:, ROWS, :], ACT.Exp).then_inc(row_exp_ready, 1)
                act.wait_ge(diffs_ready, t + 1)
                act.activation(a_mat, a_mat, ACT.Exp, scale=-1.0)
                act.activation(qk[par], qk[par], ACT.Exp).then_inc(decays_ready, 1)
                act.wait_ge(tokens_turned, t + 1)
                for h in range(DN_H):
                    k, hp = DN_H * t + h, slice(h * P, (h + 1) * P)
                    act.activation(kbe_w[par][:, hp], ps[:, K_TOK, hp], ACT.Copy, scale=col("beta_exp", k))
                    act.activation(k_rev[par][:, hp], ps[:, K_TOK, hp], ACT.Copy, scale=col("rev_exp", k))
                    ins = act.activation(vb_u[par][:, hp], ps[:, V_TOK, hp], ACT.Copy, scale=col("beta", k))
                ins.then_inc(tok_ready, 1)
                if t:
                    copy_out(2 * t - 2)
                act.wait_ge(a_turned, t + 1)
                act.activation(a_turn, ps[:, A_TURN, :], ACT.Copy).then_inc(at_ready, 1)
                if t:
                    copy_out(2 * t - 1)
                act.wait_ge(wu_ready, t + 1)
                act.activation(kbe_w[par], ps[:, W_BANK, :], ACT.Copy)
                act.activation(vb_u[par], ps[:, U_BANK, :], ACT.Copy).then_inc(wu_copied, 1)
            copy_out(2 * TT - 2)
            copy_out(2 * TT - 1)

            def merge_gates(c):
                i = (c - START["merge"]) % 4
                multiplied(act, c)
                act.activation(Z[:, 4 + 2 * i:6 + 2 * i, :], ps[:, pair(c):pair(c) + 2, :],
                               ACT.Sigmoid).then_inc(pair_free[c % 2], 1)
                head(c + 2)

            act.wait_ge(o_copied, 2 * TT)
            c0, base = START["merge"], SPLIT0["dn"]
            for m in range(2):
                for i in (2 * m, 2 * m + 1):
                    square(f"dn_out{i}", Z[:, i, :])
                merge_gates(c0 + m)
                root_table()
                for i in (2 * m, 2 * m + 1):
                    root(f"dn_out{i}", P, eps_rms)
                for i in (2 * m, 2 * m + 1):
                    act.wait_ge(gated_ready, i + 1)
                    act.activation(hh[:, i, :], NT[:, (base + i) % 2, :], ACT.Copy).then_inc(split_hi, 1)

            for m in range(4):
                c = START["merge"] + 4 * m
                if m:
                    act.wait_ge(merged_ready, m)
                    merge_gates(c)
                    merge_gates(c + 1)
                for i in (2, 3):
                    multiplied(act, c + i)
                    head(c + i + 2)
            for m in range(4):
                act.wait_ge(merged_ready, m + 1)
                for j in (2 * m, 2 * m + 1):
                    act.activation(xh[:, j, :], Y[:, j, :], ACT.Copy).then_inc(split_hi, 1)
            root_table()
            for m in range(4):
                multiplied(act, START["w_out"] + m)
                square_pair("ffn2_pre", resid, START["w_out"] + m, m)
            root("ffn2_pre", D, eps_rms)
            split_heads("ffn2_pre", lambda j: xh[:, j, :])

            def gated_block(c0, n, b=0):
                for j in range(n):
                    c = c0 + j
                    p = c % 2
                    multiplied(act, c, b * 6)
                    act.activation(Z[:, p, :], ps[:, 2 * p, :], ACT.Silu).then_inc(gate_ready, 1)
                    head(c + 2, b * 6)
                    emptied(act, c, b * 6)
                    act.activation(hh[:, j, :], Z[:, 2 + p, :], ACT.Copy).then_inc(hidden_hi, 1)
                for j in range(n, n + 4):
                    multiplied(act, c0 + j, b * 6)
                    head(c0 + j + 2, b * 6)

            with act.Fori(0, 2) as b:
                gated_block(START["ffn_2"], 8, b)
            gated_block(START["ffn_2"] + 24, FF2_TILES[2])

        @block.vector
        def _(dve):
            steps = [0]

            def step(ins):
                steps[0] += 1
                ins.then_inc(dve_step, 1)
                dve.wait_ge(dve_step, steps[0])

            def take_root(stage):
                dve.wait_ge(root_ready, STAGE_NO[stage] + 1)

            def norm_split(name, src, gain, hi, lo, n=8, stage=None, read0=None):
                take_root(stage or name)
                base = SPLIT0[name]

                def rest(j):
                    dve.wait_ge(split_hi, base + j + 1)
                    dve.tensor_tensor(lo(j), NT[:, (base + j) % 2, :], hi(j), ALU.subtract).then_inc(split_done, 1)

                for j in range(n):
                    if base + j >= 2:
                        dve.wait_ge(split_done, base + j - 1)
                    dve.scalar_tensor_tensor(out=NT[:, (base + j) % 2, :], in0=src(j), scalar=gain(j),
                                             in1=ps[:, ROOT, :], op0=ALU.mult, op1=ALU.mult).then_inc(root_read, 1)
                    if j:
                        rest(j - 1)
                rest(n - 1)

            def add_residual(stage, gain):
                take_root(stage)
                base = READS0[stage]

                def add(j):
                    dve.wait_ge(root_read, base + j + 1)
                    dve.tensor_tensor(resid[:, j, :], resid[:, j, :], Y[:, j, :], ALU.add).then_inc(resid_ready, 1)

                for j in range(DT):
                    dve.scalar_tensor_tensor(out=Y[:, j, :], in0=Y[:, j, :], scalar=gain(j), in1=ps[:, ROOT, :],
                                             op0=ALU.mult, op1=ALU.mult).then_inc(root_read, 1)
                    if j % 2:
                        add(j - 1)

            dve.memset(eps_rms, RMS_EPS).then_inc(eps_ready, 1)
            dve.memset(eps_ln, LN_EPS).then_inc(eps_ready, 1)
            dve.memset(U[:, :, 0:PAD], 0.0).then_inc(pads_zeroed, 1)
            dve.memset(small[BUCKETS:BUCKETS + 1, COLS["rel"][0]:COLS["rel"][1]], 1.0).then_inc(rel_spread, 1)
            dve.wait_ge(vecs_loaded, 16)
            dve.wait_ge(pads_zeroed, 1)
            norm_split("mix0_pre", lambda j: resid[:, j, :], lambda j: vec("mix_pre", j),
                       lambda j: xh[:, j, :], lambda j: xl[:, j, :])

            def gate(j, h=0):
                dve.wait_ge(gate_ready, h * 2 + (j + 1))
                at = j % 2
                if isinstance(h, int):
                    dst, bias_ = U[:, 2 * h + j:2 * h + j + 1, PAD:UW], vec("b_pw1", 2 * h + j)
                else:
                    dst, bias_ = U[:, bass.ds(h * 2 + j, 1), PAD:UW], PV[:, bass.ds(h * 2 + (VEC["b_pw1"] + j), 1)]
                dve.scalar_tensor_tensor(out=dst, in0=ps[:, 2 * at:2 * at + 1, :], scalar=bias_,
                                         in1=SQ[:, at:at + 1, :], op0=ALU.add, op1=ALU.mult).then_inc(pair_free[at], 1)

            def convolve(j, h=0, n_taps=DVE_TAPS):
                gated(dve, j, h)
                t = 2 * h + j if isinstance(h, int) else h * 2 + j
                even = Y[:, t:t + 1, :] if isinstance(h, int) else Y[:, bass.ds(t, 1), :]
                odd = NT[:, j:j + 1, :]
                for i in range(n_taps):
                    k = TAPS - n_taps + i
                    acc = odd if i % 2 else even
                    x = shifted(k, j, h)
                    if isinstance(h, int):
                        x = x.unsqueeze(1)
                    if i == 0:
                        dve.wait_ge(pe_taps_done, h * 2 + (j + 1))
                        was = ps[:, TAP_BANK[j]:TAP_BANK[j] + 1, :]
                    elif i == 1:
                        dve.wait_ge(products_added, h * (2 * POOL_TAPS - 2) + (j + 1) * (POOL_TAPS - 1))
                        was = pool_sum[j].unsqueeze(1)
                    else:
                        dve.wait_ge(taps_done, h * (2 * DVE_TAPS) + (j * DVE_TAPS + i - 1))
                        was = acc
                    dve.scalar_tensor_tensor(out=acc, in0=x, scalar=tap(k, j, h), in1=was,
                                             op0=ALU.mult, op1=ALU.add).then_inc(taps_done, 1)
                dve.wait_ge(taps_done, h * (2 * DVE_TAPS) + (j * DVE_TAPS + n_taps))
                b_dw = vec("b_dw", t) if isinstance(h, int) else PV[:, bass.ds(h * 2 + (VEC["b_dw"] + j), 1)]
                dve.scalar_tensor_tensor(out=even, in0=even, in1=odd, op0=ALU.add, op1=ALU.add,
                                         scalar=b_dw).then_inc(conv_ready, 1)

            gate(0)
            with dve.Fori(0, DT // 2 - 1) as h:
                gate(1, h)
                convolve(0, h)
                gate(2, h)
                convolve(1, h)
            gate(1, DT // 2 - 1)
            convolve(0, DT // 2 - 1)
            convolve(1, DT // 2 - 1, DVE_TAPS - LAST_TAPS)
            dve.wait_ge(rows_loaded, 64)
            dve.wait_ge(rel_spread, 1)
            dve.wait_ge(conv_ready, DT)
            dve.tensor_copy(rel_wide, small[0:BUCKETS + 1, COLS["rel"][0]:COLS["rel"][1]].unsqueeze(2)
                            .to_broadcast([BUCKETS + 1, SW_H, P])).then_inc(rel_spread, 1)
            dve.wait_ge(mean_summed, 1)
            step(dve.tensor_scalar(NT[:, 0, :], ps[:, SUMS, :], 1.0 / D, None, ALU.mult))
            for j in range(DT):
                dve.tensor_tensor(Y[:, j, :], Y[:, j, :], NT[:, 0, :], ALU.subtract).then_inc(centred, 1)
            take_root("ln")
            dve.wait_ge(centred, DT)
            for j in range(DT + 2):
                if j < DT:
                    dve.tensor_tensor(Y[:, j, :], Y[:, j, :], ps[:, ROOT, :], ALU.mult).then_inc(root_read, 1)
                if j >= 2:
                    dve.wait_ge(split_hi, SPLIT0["ln"] + j - 1)
                    dve.tensor_tensor(hl[:, j - 2, :], NT[:, (SPLIT0["ln"] + j - 2) % 2, :], hh[:, j - 2, :],
                                      ALU.subtract).then_inc(split_done, 1)

            def ffn(layer):
                c0 = START[f"ffn_{layer}"]
                resid_all(dve, f"mix{layer}")
                dve.memset(Y[:, :, :], 0.0).then_inc(y_zeroed, 1)
                dve.wait_ge(y_zeroed, layer + 1)
                with dve.Fori(0, FF_BLOCKS) as b:
                    for j in range(8):
                        c = c0 + j
                        p = c % 2
                        if j < 4:
                            emptied(dve, c, b * 4)
                            relu, sq = Z[:, 2 * p:2 * p + 2, :], Z[:, 4 + 2 * p:6 + 2 * p, :]
                            dve.tensor_tensor(sq, relu, relu, ALU.mult).then_inc(hidden_sq, 1)
                            dve.wait_ge(hidden_hi, b * 4 + (16 * layer + j + 1))
                            dve.tensor_tensor(hl[:, 2 * j:2 * j + 2, :], sq, hh[:, 2 * j:2 * j + 2, :],
                                              ALU.subtract).then_inc(hidden_ready, 1)
                        else:
                            multiplied(dve, c, b * 4)
                            y = Y[:, 2 * (j - 4):2 * (j - 4) + 2, :]
                            dve.tensor_tensor(y, y, ps[:, 2 * p:2 * p + 2, :], ALU.add).then_inc(pair_free[p], 1)

            add_residual("mix0_post", lambda j: vec("mix_post", j))
            norm_split("ffn0_pre", lambda j: resid[:, j, :], lambda j: vec("ffn_pre", j),
                       lambda j: xh[:, j, :], lambda j: xl[:, j, :])
            ffn(0)
            add_residual("ffn0_post", lambda j: vec("ffn_post", j))

            norm_split("mla_kv_in", lambda j: resid[:, j, :], lambda j: vec("kv_in", j), lambda j: xh[:, j, :],
                       lambda j: xl[:, j, :], stage="mla_in")
            norm_split("mla_q_in", lambda j: resid[:, j, :], lambda j: vec("mix_pre", DT + j),
                       lambda j: hh[:, j, :], lambda j: hl[:, j, :], stage="mla_in")
            norm_split("kv", lambda j: E[:, j, :], lambda j: vec("kv_norm", j), lambda j: xh[:, j, :],
                       lambda j: xl[:, j, :], 2)
            norm_split("q", lambda j: E[:, 3 + j, :], lambda j: vec("q_norm", j), lambda j: xh[:, 2 + j, :],
                       lambda j: xl[:, 2 + j, :], 3)

            dve.wait_ge(split_done, SPLIT0["q"] + 3)
            dve.wait_ge(tables_loaded, 16)
            step(dve.memset(E[:, 4:6, :], 0.0))

            def rope(r, src, dsts):
                dve.wait_ge(rotated, r + 1)
                step(dve.tensor_tensor(NT[:, 0, :], ps[:, 6 + r % 2, :], sin_t, ALU.mult))
                step(dve.tensor_tensor(NT[:, 1, :], src, cos_t, ALU.mult))
                for n, (dst, p) in enumerate(dsts):
                    ins = dve.tensor_tensor(dst, NT[p, 0, :], NT[p, 1, :], ALU.add)
                    if n < len(dsts) - 1:
                        step(ins)
                ins.then_inc(roped, 1)
                dve.wait_ge(roped, r + 1)

            rope(0, E[:, 2, :], [(E[0:ROPE, 4, :], slice(0, ROPE)), (E[ROPE:P, 5, :], slice(ROPE, P))])
            for r in range(4):
                rope(r + 1, SQ[:, r, :] if r < 2 else rope_raw[:, r - 2, :], [(E[:, r, :], slice(0, P))])

            def attend(it0, n_keys, group, name):
                def output(g):
                    j = g + (0 if it0 == 0 else 4)
                    dve.wait_ge(split_hi, SPLIT0[name] + g + 1)
                    dve.tensor_tensor(hl[:, j, :], ps[:, OUTPUT[g % 2], :], hh[:, j, :],
                                      ALU.subtract).then_inc(split_done, 1)

                def marked(ins):
                    steps[0] += 1
                    ins.then_inc(dve_step, 1)
                    return steps[0]

                for it in range(it0, it0 + 34):
                    k, n, bank = it % 8, it - it0, SCORE[it % 4]
                    now, before = n < 32, n >= 2
                    nk = n_keys(n) if now else 0
                    kb = (it - 2) % 8
                    if now:
                        dve.wait_ge(scores_ready, it + 1)
                        if it0 == 0:
                            masked = marked(dve.memset(ps[0:DN_CH, bank, nk - DN_CH:nk], -BIG))
                        else:
                            masked = marked(dve.scalar_tensor_tensor(
                                out=ps[:, bank, 0:nk], in0=ps[:, bank, 0:nk], scalar=SW_D ** -0.5,
                                in1=bias[:, n // 4, 2 * P - nk:2 * P], op0=ALU.mult, op1=ALU.add))
                    if before:
                        dve.wait_ge(probs_ready, it - 1)
                        if it0:
                            summed = marked(dve.tensor_tensor(col("row_sum", kb), col("row_sum", kb),
                                                              col("sink_exp", kb), ALU.add))
                    if now:
                        dve.wait_ge(dve_step, masked)
                        largest = marked(dve.reduce_max(col("max", k), ps[:, bank, 0:nk], AX_X))
                    if before:
                        if it0:
                            dve.wait_ge(dve_step, summed)
                        inverted = marked(dve.reciprocal(col("inv_sum", kb), col("row_sum", kb)))
                    if now:
                        dve.wait_ge(dve_step, largest)
                        if it0 == 0:
                            dve.tensor_scalar(col("neg_max", k), col("max", k), -(QKD ** -0.5), None,
                                              ALU.mult).then_inc(max_ready, 1)
                        else:
                            dve.tensor_scalar(col("neg_max", k), col("max", k), col("sinks", n // 4), -1.0, ALU.max,
                                              ALU.mult).then_inc(max_ready, 1)
                    if before:
                        dve.wait_ge(dve_step, inverted)
                        if it >= 4:
                            dve.wait_ge(probs_turned, it - 3)
                        nb = n_keys(n - 2)
                        dve.tensor_scalar(NT[:, it % 2, 0:nb], ps[:, SCORE[(it - 2) % 4], 0:nb], col("inv_sum", kb),
                                          None, ALU.mult).then_inc(probs_scaled, 1)
                    if n - 4 >= group and (n - 4) % group == 0:
                        output((n - 4) // group - 1)
                output(32 // group - 1)

            attend(0, lambda n: (n % 4 + 1) * P, 4, "heads")
            add_residual("mix1_post", lambda j: vec("mix_post", DT + j))
            norm_split("ffn1_pre", lambda j: resid[:, j, :], lambda j: vec("ffn_pre", DT + j),
                       lambda j: xh[:, j, :], lambda j: xl[:, j, :])
            ffn(1)
            add_residual("ffn1_post", lambda j: vec("ffn_post", DT + j))

            norm_split("attn2", lambda j: resid[:, j, :], lambda j: vec("attn_norm", j),
                       lambda j: xh[:, j, :], lambda j: xl[:, j, :])
            dve.wait_ge(ba_ready, 1)
            ba = cols("ba").rearrange("p (t n) -> p t n", n=8)

            def by_tile(name):
                return cols(name).rearrange("p (t n) -> p t n", n=DN_H)

            def all_tiles(name):
                return cols(name).unsqueeze(1).to_broadcast([P, TT, DN_H])

            dve.tensor_tensor(by_tile("dt_in"), ba[:, :, DN_H:2 * DN_H], all_tiles("dt_bias"),
                              ALU.add).then_inc(softplus_in, 1)
            dve.wait_ge(softplus_out, 2)
            step(dve.scalar_tensor_tensor(out=cols("soft"), in0=cols("dt_in"), scalar=0.0, in1=cols("soft"),
                                          op0=ALU.max, op1=ALU.add))
            dve.scalar_tensor_tensor(out=by_tile("decay"), in0=by_tile("soft"), scalar=-1.0,
                                     in1=all_tiles("a_exp"), op0=ALU.mult, op1=ALU.mult).then_inc(decay_ready, 1)
            for i in range(4):
                take_root(f"swa_q{i}")
                dve.scalar_tensor_tensor(out=Y[:, i, :], in0=Y[:, i, :], scalar=vec("swa_q"),
                                         in1=ps[:, STAT_BANKS[f"swa_q{i}"][1], :],
                                         op0=ALU.mult, op1=ALU.mult).then_inc(root_read, 1)
            for i in range(2):
                take_root(f"swa_k{i}")
                rt = STAT_BANKS[f"swa_k{i}"][1]
                up, down = Y[:, 4 + 2 * i, :], Y[:, 5 + 2 * i, :]
                step(dve.memset(down[0:SW_D, :], 0.0))
                step(dve.scalar_tensor_tensor(out=down[SW_D:P, :], in0=up[SW_D:P, :], scalar=vec("swa_k")[SW_D:P, :],
                                              in1=ps[SW_D:P, rt, :], op0=ALU.mult, op1=ALU.mult))
                step(dve.scalar_tensor_tensor(out=up[0:SW_D, :], in0=up[0:SW_D, :], scalar=vec("swa_k")[0:SW_D, :],
                                              in1=ps[0:SW_D, rt, :], op0=ALU.mult, op1=ALU.mult))
                dve.memset(up[SW_D:P, :], 0.0).then_inc(root_read, 1)
            dve.wait_ge(bias_loaded, 16 * SW_H)
            attend(32, lambda n: P if n % 4 == 0 else 2 * P, 8, "swa")

            dve.memset(raw4[:, :, 0:DN_TAPS - 1], 0.0).then_inc(pads_zeroed, 1)
            dve.wait_ge(pads_zeroed, 2)
            for m in range(6):
                emptied(dve, START["qkv"] + m)
                for k in range(DN_TAPS):
                    for n in range(2):
                        t = 2 * m + n
                        w, src = vec("dn_conv", 12 * k + t), raw4[:, 2 * (m % 2) + n, k:k + SEQ]
                        if k:
                            dve.wait_ge(dn_taps_done, 6 * m + 2 * (k - 1) + n + 1)
                            ins = dve.scalar_tensor_tensor(out=Z[:, t, :], in0=src, scalar=w, in1=Z[:, t, :],
                                                           op0=ALU.mult, op1=ALU.add)
                        else:
                            ins = dve.tensor_scalar(Z[:, t, :], src, w, None, ALU.mult)
                        ins.then_inc(dn_conv_ready if k == DN_TAPS - 1 else dn_taps_done, 1)
                if 1 <= m <= 4:
                    for i in (2 * m - 2, 2 * m - 1):
                        take_root(f"dn_in{i}")
                        dve.tensor_tensor(Z[:, i, :], Z[:, i, :], ps[:, STAT_BANKS[f"dn_in{i}"][1], :],
                                          ALU.mult).then_inc(root_read, 1)

            dve.wait_ge(decay_exps, 1)
            dve.tensor_tensor(cols("beta_exp"), cols("beta"), cols("cum_exp"), ALU.mult).then_inc(beta_exp_ready, 1)
            dve.wait_ge(consts_loaded, 16)
            dve.wait_ge(root_read, READS0["dn_in7"] + 1)
            step(dve.memset(state, 0.0))
            ident_h = bcast_heads(ident)

            def new_values(n):
                r = slice(n % 2 * DN_CH, (n % 2 + 1) * DN_CH)
                dve.wait_ge(ws_ready, n + 1)
                dve.tensor_tensor(v_new[r, :], vb_u[n // 2 % 2][r, :], ps[r, WS, :], ALU.subtract).then_inc(new_ready, 1)

            def new_state(n):
                dve.wait_ge(o_ready, n + 1)
                for h in range(DN_H):
                    hp = slice(h * P, (h + 1) * P)
                    ins = dve.scalar_tensor_tensor(out=state[:, hp], in0=state[:, hp],
                                                   scalar=col("state_decay", n // 2 % 2 * 8 + 2 * h + n % 2),
                                                   in1=ps[:, STATE, hp], op0=ALU.mult, op1=ALU.add)
                ins.then_inc(state_ready, 1)

            def halves(t):
                return t.rearrange("p (h n) -> p h n", n=P)

            for t in range(TT):
                par = t % 2
                tok = slice(t * P, (t + 1) * P)
                k0 = COLS["decay"][0] + DN_H * t
                dve.tensor_copy(by_head(spread), small[:, k0:k0 + DN_H].unsqueeze(2)
                                .to_broadcast([P, DN_H, P])).then_inc(spread_ready, 1)
                dve.wait_ge(row_exp_ready, t + 1)
                for h in range(DN_H):
                    hp = slice(h * P, (h + 1) * P)
                    dve.scalar_tensor_tensor(out=a_mat[:, hp], in0=ps[:, ROWS, hp], scalar=col("cum", DN_H * t + h),
                                             in1=const("decay_mask"), op0=ALU.subtract, op1=ALU.add)
                    ins = dve.scalar_tensor_tensor(out=qk[par][:, hp], in0=ps[:, ROWS, hp],
                                                   scalar=col("cum", DN_H * t + h), in1=const("decay_mask_t"),
                                                   op0=ALU.subtract, op1=ALU.add)
                ins.then_inc(diffs_ready, 1)
                c0 = COLS["state_decay"][0] + 8 * par
                dve.tensor_copy(small[:, c0:c0 + 8], row_exp[:, DN_CH - 1:SEQ:DN_CH])
                dve.scalar_tensor_tensor(out=by_head(q_exp[par]), in0=Z[:, 0:DN_H, tok], scalar=float(P) ** -0.5,
                                         in1=by_head(row_exp), op0=ALU.mult, op1=ALU.mult).then_inc(qe_ready, 1)
                if t:
                    new_values(2 * t - 2)
                dve.wait_ge(decays_ready, t + 1)
                dve.wait_ge(products_ready, t + 1)
                for h in range(DN_H):
                    hp = slice(h * P, (h + 1) * P)
                    ins = dve.scalar_tensor_tensor(out=a_mat[:, hp], in0=ps[:, KK, hp], scalar=col("beta", DN_H * t + h),
                                                   in1=a_mat[:, hp], op0=ALU.mult, op1=ALU.mult)
                ins.then_inc(a_ready, 1)
                dve.scalar_tensor_tensor(out=qk[par], in0=ps[:, KQ, :], scalar=float(P) ** -0.5, in1=qk[par],
                                         op0=ALU.mult, op1=ALU.mult).then_inc(qk_ready, 1)
                if t:
                    new_state(2 * t - 2)
                dve.wait_ge(a_ready, t + 1)
                for lv in range(6):
                    mask = const("inv_mask")[:, lv * P:(lv + 1) * P].unsqueeze(1).to_broadcast([P, 2, P])
                    for g in range(2):
                        hs = slice(g * HALF, (g + 1) * HALF)
                        if lv:
                            dve.wait_ge(level_p, 10 * t + 2 * lv + g - 1)
                            src = ps[:, LEVEL_P[g], 0:HALF]
                        else:
                            src = a_mat[:, hs]
                        dve.tensor_tensor(halves(level_mask[:, hs]), halves(src), mask, ALU.mult).then_inc(level_m, 1)
                    if lv == 0:
                        dve.wait_ge(level_m, 12 * t + 2)
                        for g in range(2):
                            dve.tensor_tensor(halves(inverse[g][:, 0:HALF]), ident_h[:, 0:2, :],
                                              halves(level_mask[:, g * HALF:(g + 1) * HALF]), ALU.subtract)
                        if t:
                            new_values(2 * t - 1)
                    for g in range(2):
                        dve.wait_ge(level_qr, 12 * t + 2 * lv + g + 1)
                        part = slice(0 if 0 < lv < 5 else HALF, SEQ)
                        was = inverse[g][:, part] if lv else ident_h[:, 0:2, :]
                        new, less = inverse[g][:, part], ps[:, LEVEL_QR[g], part]
                        if lv == 0:
                            new, less = halves(new), halves(less)
                        dve.tensor_tensor(new, was, less, ALU.subtract).then_inc(level_t, 1)
                    if lv == 0 and t:
                        new_state(2 * t - 1)
                dve.wait_ge(level_t, 12 * (t + 1))
            for n in (2 * TT - 2, 2 * TT - 1):
                new_values(n)
                new_state(n)
            base = SPLIT0["dn"]

            def gated_rest(i):
                dve.wait_ge(split_hi, base + i + 1)
                dve.tensor_tensor(hl[:, i, :], NT[:, (base + i) % 2, :], hh[:, i, :],
                                  ALU.subtract).then_inc(split_done, 1)

            for i in range(DN_H):
                take_root(f"dn_out{i}")
                dve.scalar_tensor_tensor(out=Z[:, i, :], in0=Z[:, i, :], scalar=vec("dn_out"),
                                         in1=ps[:, STAT_BANKS[f"dn_out{i}"][1], :],
                                         op0=ALU.mult, op1=ALU.mult).then_inc(root_read, 1)
                dve.wait_ge(root_read, READS0[f"dn_out{i}"] + 1)
                dve.wait_ge(split_done, base + i - 1)
                dve.tensor_tensor(NT[:, (base + i) % 2, :], Z[:, i, :], Z[:, 12 + i, :],
                                  ALU.mult).then_inc(gated_ready, 1)
                if i:
                    gated_rest(i - 1)
            gated_rest(DN_H - 1)
            for m in range(4):
                c = START["merge"] + 4 * m
                y, term = Y[:, 2 * m:2 * m + 2, :], Z[:, 8:10, :]
                emptied(dve, c)
                emptied(dve, c + 1)
                multiplied(dve, c + 2)
                dve.tensor_tensor(y, ps[:, pair(c + 2):pair(c + 2) + 2, :], Z[:, 4:8:2, :],
                                  ALU.mult).then_inc(pair_free[c % 2], 1)
                multiplied(dve, c + 3)
                if m:
                    dve.wait_ge(merged_ready, m)
                dve.tensor_tensor(term, ps[:, pair(c + 3):pair(c + 3) + 2, :], Z[:, 5:8:2, :],
                                  ALU.mult).then_inc(pair_free[(c + 1) % 2], 1)
                emptied(dve, c + 2)
                emptied(dve, c + 3)
                dve.tensor_tensor(y, y, term, ALU.add).then_inc(merged_ready, 1)
            for j in range(DT):
                dve.wait_ge(split_hi, SPLIT0["merged"] + j + 1)
                dve.tensor_tensor(xl[:, j, :], Y[:, j, :], xh[:, j, :], ALU.subtract).then_inc(split_done, 1)

            def add_output(c, m, h=0):
                multiplied(dve, c, h)
                r = resid[:, 2 * m:2 * m + 2, :]
                dve.tensor_tensor(r, r, ps[:, pair(c):pair(c) + 2, :], ALU.add).then_inc(pair_free[c % 2], 1)

            for m in range(4):
                add_output(START["w_out"] + m, m)
            for m in range(4):
                emptied(dve, START["w_out"] + m)
            norm_split("ffn2_pre", lambda j: resid[:, j, :], lambda j: vec("ffn_norm", j),
                       lambda j: xh[:, j, :], lambda j: xl[:, j, :])

            def gated_block(c0, n, b=0, base=0):
                for j in range(n):
                    c = c0 + j
                    p = c % 2
                    dve.wait_ge(gate_ready, b * 8 + (8 + base + j + 1))
                    dve.tensor_tensor(Z[:, 2 + p, :], ps[:, 2 * p + 1, :], Z[:, p, :],
                                      ALU.mult).then_inc(pair_free[p], 1)
                    dve.wait_ge(hidden_hi, b * 8 + (32 + base + j + 1))
                    dve.tensor_tensor(hl[:, j, :], Z[:, 2 + p, :], hh[:, j, :], ALU.subtract).then_inc(hidden_ready, 1)
                for m in range(4):
                    c = c0 + n + m
                    multiplied(dve, c, b * 6)
                    r = resid[:, 2 * m:2 * m + 2, :]
                    dve.tensor_tensor(r, r, ps[:, pair(c):pair(c) + 2, :], ALU.add).then_inc(pair_free[c % 2], 1)

            dve.wait_ge(split_done, SPLIT0["ffn2_pre"] + DT)
            with dve.Fori(0, 2) as b:
                gated_block(START["ffn_2"], 8, b)
            gated_block(START["ffn_2"] + 24, FF2_TILES[2], 0, 16)

        @block.tensor
        def _(pe):
            def stats(stage, weights=ones, tiles=None):
                n, base = SQUARES[stage], SQUARES0[stage]
                tiles = tiles or range(n)
                if ROOTS_BEFORE[stage] and tiles[0] == 0:
                    pe.wait_ge(root_ready, ROOTS_BEFORE[stage])
                for j in tiles:
                    pe.wait_ge(squares_ready, base + j + 1)
                    pe.matmul(ps[:, STAT_BANKS[stage][0], :], weights, SQ[:, (base + j) % 2, :], start=j == 0,
                              stop=j == n - 1).then_inc(squares_summed, 1)

            def post_stats(stage, m):
                if m < 3 and m:
                    stats(stage, tiles=range(2 * m - 2, 2 * m))
                if m == 3:
                    stats(stage, tiles=range(6, DT))

            def late_stats(stage, m):
                return (lambda: stats(stage, tiles=range(4, 6))) if m == 3 else None

            def start_chunk(c, h=0):
                pe.wait_ge(lo_ready, h * 2 + (c + 1))
                if c >= 2:
                    pe.wait_ge(pair_free[c % 2], h + c // 2)

            def passes(hi, lo, whi_, wlo_):
                return ((whi_, hi), (whi_, lo), (wlo_, hi))

            def project(c, hi, lo, h=0, k_tiles=DT, k0=0, need=None, second=None, second_need=None,
                        paired=True, midway=None):
                start_chunk(c, h)
                p = c % 2
                order = ([(n, k) for k in range(k_tiles) for n in range(2)] if need and paired else
                         [(n, k) for n in range(2) for k in range(k_tiles)])
                for n, k in order:
                    if midway and (n, k) == (1, 0):
                        midway()
                    if n and second:
                        hi, lo = second
                    if need and n == 0:
                        need(k)
                    if second_need and n == 1:
                        second_need(k)
                    w = slice(k * 2 * P + n * P, k * 2 * P + (n + 1) * P)
                    for q, (wt, xt) in enumerate(passes(hi, lo, whi, wlo)):
                        ins = pe.matmul(ps[:, 2 * p + n, :], wt[:, p, w], xt[:, k0 + k, :],
                                        start=k == 0 and q == 0, stop=k == k_tiles - 1 and q == 2)
                ins.then_inc(chunk_done, 1)

            def operand(name):
                return lambda k: pe.wait_ge(split_done, SPLIT0[name] + k + 1)

            def project_tokens(c, k_tiles, n_out, need=None):
                start_chunk(c)
                p = c % 2
                per_bank = 2
                for t in range(TT):
                    dst = ps[:, 2 * p + t // per_bank, (t % per_bank) * n_out:(t % per_bank + 1) * n_out]
                    for k in range(k_tiles):
                        if need and t == 0:
                            need(k)
                        for q, (xt, wt) in enumerate(((xh, whi), (xh, wlo), (xl, whi))):
                            ins = pe.matmul(dst, xt[:, k, t * P:(t + 1) * P], wt[:, p, k * n_out:(k + 1) * n_out],
                                            start=k == 0 and q == 0, stop=k == k_tiles - 1 and q == 2)
                ins.then_inc(chunk_done, 1)

            pe.wait_ge(ones_loaded, 16)
            stats("mix0_pre")
            c0 = START["pw1"]
            project(c0, xh, xl, need=operand("mix0_pre"))
            project(c0 + 1, xh, xl)

            def taps(j, h=0, more=0):
                at = j % 2
                pe.wait_ge(diag_ready, h * 2 + (j + 1))
                gated(pe, j, h)
                weights = [(k, diag[at][k]) for k in range(PE_TAPS)]
                weights += [(PE_TAPS + POOL_TAPS + i, last_diag[i]) for i in range(more)]
                for n, (k, w) in enumerate(weights):
                    ins = pe.matmul(ps[:, TAP_BANK[at], :], w, shifted(k, j, h), start=n == 0,
                                    stop=n == len(weights) - 1)
                ins.then_inc(pe_taps_done, 1)

            taps(0)
            with pe.Fori(0, DT // 2 - 1) as h:
                project(c0 + 2, xh, xl, h)
                taps(1, h)
                project(c0 + 3, xh, xl, h)
                taps(2, h)
            taps(1, DT // 2 - 1, LAST_TAPS)
            pe.wait_ge(root_ready, 1)
            for j in range(DT):
                pe.wait_ge(conv_ready, j + 1)
                ins = pe.matmul(ps[:, SUMS, :], ones, Y[:, j, :], start=j == 0, stop=j == DT - 1)
            ins.then_inc(mean_summed, 1)
            stats("ln")
            c0 = START["pw2"]
            for c in range(c0, c0 + 4):
                project(c, hh, hl, need=operand("ln") if c == c0 else None, midway=late_stats("mix0_post", c - c0))
                post_stats("mix0_post", c - c0)

            def ffn(layer, name):
                c0 = START[f"ffn_{layer}"]

                def block_of(b, last=False):
                    for j in range(4):
                        project(c0 + j, xh, xl, b * 4, need=operand(name) if j == 0 else None)
                    for j in range(4, 8):
                        project(c0 + j, hh, hl, b * 4, need=(lambda k: pe.wait_ge(
                            hidden_ready, b * 4 + (16 * layer + k // 2 + 1)) if k % 2 == 0 else None)
                            if j == 4 else None, midway=late_stats(f"ffn{layer}_post", j - 4) if last else None)
                        if last:
                            post_stats(f"ffn{layer}_post", j - 4)

                pe.wait_ge(split_done, SPLIT0[name] + 1)
                with pe.Fori(0, FF_BLOCKS - 1) as b:
                    block_of(b)
                block_of(FF_BLOCKS - 1, True)

            pe.wait_ge(rel_spread, 2)
            pe.wait_ge(onehot_loaded, 16)
            for h in range(SW_H):
                if h >= 2:
                    pe.wait_ge(rel_copied, h - 1)
                pe.matmul(ps[:, 6 + h % 2, 0:RELW], rel_wide[:, h, :], onehot, start=True,
                          stop=True).then_inc(rel_summed, 1)
            stats("ffn0_pre")
            ffn(0, "ffn0_pre")

            stats("mla_in")
            c = START["latent"]
            project(c, xh, xl, need=operand("mla_kv_in"))
            project(c + 1, xh, xl, second=(hh, hl), second_need=operand("mla_q_in"))
            stats("kv")
            project(c + 2, hh, hl)
            emptied(pe, c + 1)
            pe.wait_ge(tables_loaded, 16)
            pe.matmul(ps[:, 6, :], rotate, E[:, 2, :], start=True, stop=True).then_inc(rotated, 1)
            for m in range(4):
                project(START["uk"] + m, xh, xl, k_tiles=2, need=operand("kv") if m == 0 else None)
                if m == 1:
                    stats("q")
            for m in range(6):
                project(START["uq"] + m, xh, xl, k_tiles=3, k0=2, need=operand("q") if m == 0 else None)
            for r in range(4):
                if r == 0:
                    emptied(pe, START["uq"] + 4)
                if r == 2:
                    emptied(pe, START["uq"] + 5)
                if r >= 1:
                    pe.wait_ge(roped, r)
                pe.matmul(ps[:, 6 + (r + 1) % 2, :], rotate, SQ[:, r, :] if r < 2 else rope_raw[:, r - 2, :],
                          start=True, stop=True).then_inc(rotated, 1)
            for m in range(4):
                project_tokens(START["uv"] + m, 2, 256)
            for m in range(2):
                emptied(pe, START["wo"] - 1 - m)
            pe.wait_ge(roped, 5)
            pe.wait_ge(root_ready, STAGE_NO["q"] + 1)
            pe.wait_ge(root_read, READS0["q"] + 3)

            def attend(it0, n_keys, group, name, score, values):
                def scores(it):
                    if it - it0 >= 4:
                        pe.wait_ge(probs_scaled, it - 3)
                    score(it - it0, ps[:, SCORE[it % 4], :]).then_inc(scores_ready, 1)

                def turn(it):
                    pe.wait_ge(probs_scaled, it + 1)
                    if it >= 2:
                        pe.wait_ge(probs_back, it - 1)
                    for j in range(n_keys(it - it0) // P):
                        ins = pe.transpose(ps[:, TURN[it % 2], j * P:(j + 1) * P], NT[:, it % 2, j * P:(j + 1) * P],
                                           ident)
                    ins.then_inc(probs_turned, 1)

                def times_values(it):
                    blocks = n_keys(it - it0) // P
                    pe.wait_ge(probs_back, it + 1)
                    g = (it - it0) // group
                    if (it - it0) % group == 0 and g >= 2:
                        pe.wait_ge(split_done, SPLIT0[name] + g - 1)
                    dst, lhs = values(it - it0, ps[:, OUTPUT[g % 2], :])
                    for j in range(blocks):
                        ins = pe.matmul(dst, lhs(j), SQ[:, it % 2, j * P:(j + 1) * P], start=j == 0,
                                        stop=j == blocks - 1)
                    ins.then_inc(pv_done, 1)

                for it in range(it0, it0 + 3):
                    scores(it)
                for it in range(it0, it0 + 32):
                    if it + 3 < it0 + 32:
                        scores(it + 3)
                    turn(it)
                    if it > it0:
                        times_values(it - 1)
                times_values(it0 + 31)

            def mla_score(n, bank):
                h, i = n // 4, n % 4
                q, nk = slice(i * P, (i + 1) * P), (i + 1) * P
                pe.matmul(bank[:, 0:nk], Y[:, h, q], Z[:, h, 0:nk], start=True, stop=False)
                return pe.matmul(bank[:, 0:nk], E[:, h // 2, q], E[:, 4 + h % 2, 0:nk], start=False, stop=True)

            attend(0, lambda n: (n % 4 + 1) * P, 4, "heads", mla_score,
                   lambda n, bank: (bank[:, (n % 4) * P:(n % 4 + 1) * P],
                                    lambda j: V[:, j, (n // 4) * P:(n // 4 + 1) * P]))
            for m in range(4):
                project(START["wo"] + m, hh, hl, need=operand("heads") if m == 0 else None,
                        paired=False,
                        midway=late_stats("mix1_post", m))
                post_stats("mix1_post", m)
            stats("ffn1_pre")
            ffn(1, "ffn1_pre")

            stats("attn2")
            for m in range(2):
                project(START["sq"] + m, xh, xl, need=operand("attn2") if m == 0 else None)
            project(START["sk"], xh, xl)
            pe.wait_ge(consts_loaded, 16)
            stats("swa_q0", half_ones)
            project_tokens(START["sv_ba"], DT, P + 8)
            stats("swa_q1", half_ones)
            for m in range(2):
                project(START["z"] + m, xh, xl)
                stats(f"swa_q{m + 2}", half_ones)
            for i in range(2):
                stats(f"swa_k{i}", half_ones)
            for k in range(2):
                emptied(pe, START["z"] + k)
            emptied(pe, START["sv_ba"])
            pe.wait_ge(root_read, READS0["swa_k1"] + 1)

            def swa_score(n, bank):
                h, i = n // 4, n % 4
                nk = P if i == 0 else 2 * P
                keys = slice(max(i - 1, 0) * P, (i + 1) * P)
                return pe.matmul(bank[:, 0:nk], Y[:, h // 2, i * P:(i + 1) * P],
                                 Y[:, 4 + 2 * (h // 4) + h % 2, keys], start=True, stop=True)

            def swa_values(n, bank):
                h, i = n // 4, n % 4
                r = slice((h % 2) * SW_D, (h % 2 + 1) * SW_D)
                b0 = max(i - 1, 0)
                return (bank[r, i * P:(i + 1) * P],
                        lambda j: sv_tok[:, (b0 + j) * P + (h // 4) * SW_D:(b0 + j) * P + (h // 4 + 1) * SW_D])

            attend(32, lambda n: P if n % 4 == 0 else 2 * P, 8, "swa", swa_score, swa_values)
            pe.wait_ge(split_done, SPLIT0["swa"] + 4)

            for m in range(6):
                if m == 0:
                    pe.wait_ge(decay_ready, 1)
                    pe.matmul(ps[:, 6, 0:16], const("tri"), cols("decay"), start=True, stop=True)
                    pe.matmul(ps[:, 6, 16:32], const("rev"), cols("decay"), start=True,
                              stop=True).then_inc(decay_summed, 1)
                project(START["qkv"] + m, xh, xl)
                if m == 1:
                    pe.wait_ge(decay_exps, 1)
                if 1 <= m <= 4:
                    for i in (2 * m - 2, 2 * m - 1):
                        stats(f"dn_in{i}")
            pe.wait_ge(root_read, READS0["dn_in7"] + 1)
            pe.wait_ge(dn_silu_ready, 4)
            for k in range(2):
                emptied(pe, START["merge"] - 1 - k)
            heads = [(h, slice(h * P, (h + 1) * P)) for h in range(DN_H)]

            def w_state(n):
                r, par = slice(n % 2 * DN_CH, (n % 2 + 1) * DN_CH), n // 2 % 2
                if n % 2 == 0:
                    pe.wait_ge(wu_copied, n // 2 + 1)
                if n:
                    pe.wait_ge(state_ready, n)
                for h, hp in heads:
                    ins = pe.matmul(ps[r, WS, hp], kbe_w[par][:, h * P + n % 2 * DN_CH:h * P + (n % 2 + 1) * DN_CH],
                                    state[:, hp], start=True, stop=True)
                ins.then_inc(ws_ready, 1)

            def chunk_out(n):
                r, par = slice(n % 2 * DN_CH, (n % 2 + 1) * DN_CH), n // 2 % 2
                if n % 2 == 0:
                    pe.wait_ge(qe_ready, n // 2 + 1)
                    pe.wait_ge(qk_ready, n // 2 + 1)
                if n:
                    pe.wait_ge(o_copied, n)
                pe.wait_ge(new_ready, n + 1)
                for h, hp in heads:
                    pe.matmul(ps[:, STATE, hp], k_rev[par][r, hp], v_new[r, hp], start=True, stop=True)
                for h, hp in heads:
                    cs = slice(h * P + n % 2 * DN_CH, h * P + (n % 2 + 1) * DN_CH)
                    dst = ps[:, OUT, h * DN_CH:(h + 1) * DN_CH]
                    pe.matmul(dst, state[:, hp], q_exp[par][:, cs], start=True, stop=False)
                    ins = pe.matmul(dst, v_new[r, hp], qk[par][r, cs], start=False, stop=True)
                ins.then_inc(o_ready, 1)

            for t in range(TT):
                par = t % 2
                tok = slice(t * P, (t + 1) * P)

                def rows():
                    pe.wait_ge(spread_ready, t + 1)
                    for h, hp in heads:
                        ins = pe.matmul(ps[:, ROWS, hp], spread[:, hp], const("tri"), start=True, stop=True)
                    ins.then_inc(rows_summed, 1)

                if t:
                    rows()
                    w_state(2 * t - 2)
                    pe.wait_ge(level_t, 12 * t)
                for h, hp in heads:
                    pe.matmul(ps[:, KK, hp], Z[:, DN_H + h, tok], Z[:, DN_H + h, tok], start=True, stop=True)
                for h, hp in heads:
                    ins = pe.matmul(ps[:, KQ, hp], Z[:, DN_H + h, tok], Z[:, h, tok], start=True, stop=True)
                ins.then_inc(products_ready, 1)
                for h, hp in heads:
                    pe.transpose(ps[:, K_TOK, hp], Z[:, DN_H + h, tok], ident)
                if t == 0:
                    rows()
                    pe.wait_ge(dn_silu_ready, 6)
                for h, hp in heads:
                    ins = pe.transpose(ps[:, V_TOK, hp], Z[:, 2 * DN_H + h, tok], ident)
                ins.then_inc(tokens_turned, 1)
                if t:
                    chunk_out(2 * t - 2)
                pe.wait_ge(a_ready, t + 1)
                for h, hp in heads:
                    ins = pe.transpose(ps[:, A_TURN, hp], a_mat[:, hp], ident)
                ins.then_inc(a_turned, 1)
                if t:
                    w_state(2 * t - 1)
                pe.wait_ge(qk_ready, t + 1)
                for lv in range(6):
                    if lv == 1:
                        pe.wait_ge(at_ready, t + 1)
                        pe.wait_ge(tok_ready, t + 1)
                    if lv:
                        for g in range(2):
                            pe.wait_ge(level_t, 12 * t + 2 * lv + g - 1)
                            for i in range(2):
                                hp = slice((2 * g + i) * P, (2 * g + i + 1) * P)
                                ip = slice(i * P, (i + 1) * P)
                                ins = pe.matmul(ps[:, LEVEL_P[g], ip], a_turn[:, hp], inverse[g][:, ip],
                                                start=True, stop=True)
                            ins.then_inc(level_p, 1)
                    for g in range(2):
                        pe.wait_ge(level_m, 12 * t + 2 * lv + g + 1)
                        for i in range(2):
                            hp = slice((2 * g + i) * P, (2 * g + i + 1) * P)
                            ip, up = slice(i * P, (i + 1) * P), slice(HALF + i * P, HALF + (i + 1) * P)
                            if 0 < lv < 5:
                                pe.matmul(ps[:, LEVEL_QR[g], ip], inverse[g][:, up], level_mask[:, hp],
                                          start=True, stop=True)
                            ins = pe.matmul(ps[:, LEVEL_QR[g], up], level_mask[:, hp],
                                            inverse[g][:, up] if lv else ident, start=True, stop=True)
                        ins.then_inc(level_qr, 1)
                    if lv == 0 and t:
                        chunk_out(2 * t - 1)
                for h, hp in heads:
                    if h % 2 == 0:
                        pe.wait_ge(level_t, 12 * t + 11 + h // 2)
                    up = slice(HALF + h % 2 * P, HALF + (h % 2 + 1) * P)
                    pe.matmul(ps[:, W_BANK, hp], kbe_w[par][:, hp], inverse[h // 2][:, up], start=True, stop=True)
                    ins = pe.matmul(ps[:, U_BANK, hp], inverse[h // 2][:, up], vb_u[par][:, hp], start=True, stop=True)
                ins.then_inc(wu_ready, 1)
            for n in (2 * TT - 2, 2 * TT - 1):
                w_state(n)
                chunk_out(n)
            pe.wait_ge(state_ready, 2 * TT)
            for m in range(2):
                project(START["merge"] + m, xh, xl)
                for i in (2 * m, 2 * m + 1):
                    stats(f"dn_out{i}")
            for m in range(4):
                c = START["merge"] + 4 * m
                if m:
                    project(c, xh, xl)
                    project(c + 1, xh, xl)
                project(c + 2, hh, hl, k_tiles=4, need=operand("dn") if m == 0 else None)
                project(c + 3, hh, hl, k_tiles=4, k0=4)
            for m in range(4):
                project(START["w_out"] + m, xh, xl, need=operand("merged") if m == 0 else None,
                        midway=late_stats("ffn2_pre", m))
                post_stats("ffn2_pre", m)
            pe.wait_ge(split_done, SPLIT0["ffn2_pre"] + 1)

            def gated_block(c0, n, b=0, base=0):
                for j in range(n):
                    project(c0 + j, xh, xl, b * 6, need=operand("ffn2_pre") if j == 0 and base == 0 else None)
                for m in range(4):
                    project(c0 + n + m, hh, hl, b * 6, k_tiles=n, need=(lambda k: pe.wait_ge(
                        hidden_ready, b * 8 + (32 + base + k + 1))) if m == 0 else None)

            with pe.Fori(0, 2) as b:
                gated_block(START["ffn_2"], 8, b)
            gated_block(START["ffn_2"] + 24, FF2_TILES[2], 0, 16)


def pack(inputs):
    import numpy as np
    a = {n: np.asarray(v) for n, v in inputs.items()}
    stream = np.zeros((N_CHUNK, P, CW), np.float32)

    def put(c, w):
        k, n = w.shape[0] // P, w.shape[1]
        stream[c, :, 0:k * n] = w.reshape(k, P, n).transpose(1, 0, 2).reshape(P, k * n)

    def beside(*parts):
        return np.concatenate(parts, axis=1)

    c = START["pw1"]
    w = a["conv_w_pw1"][0]
    for j in range(8):
        put(c + j, beside(w[:, j * P:(j + 1) * P], w[:, D + j * P:D + (j + 1) * P]))
    for name, w, n in (("pw2", a["conv_w_pw2"][0], 4), ("wo", a["mla_w_o"][0], 4), ("w_out", a["w_out_2"][0], 4),
                       ("uk", a["kv_w_uk"], 4), ("uv", a["kv_w_uv"], 4)):
        for j in range(n):
            put(START[name] + j, w[:, j * 256:(j + 1) * 256])
    for layer in range(2):
        c = START[f"ffn_{layer}"]
        w1, w2 = a["w_ff1"][layer], a["w_ff2"][layer]
        for b in range(FF_BLOCKS):
            for j in range(4):
                put(c + 8 * b + j, w1[:, b * D + j * 256:b * D + (j + 1) * 256])
                put(c + 8 * b + 4 + j, w2[b * D:(b + 1) * D, j * 256:(j + 1) * 256])
    c = START["latent"]
    kr, dq = a["kv_w_kr"], a["mla_w_dq"][0]
    put(c, a["kv_w_dkv"])
    put(c + 1, beside(kr, kr, dq[:, 0:P]))
    put(c + 2, dq[:, P:3 * P])
    c, w = START["uq"], a["mla_w_uq"][0].reshape(Q_LORA, NH, QKD)
    for m in range(4):
        put(c + m, w[:, 2 * m:2 * m + 2, 0:NOPE].reshape(Q_LORA, 256))
    for m in range(2):
        put(c + 4 + m, w[:, 4 * m:4 * m + 4, NOPE:QKD].reshape(Q_LORA, 256))
    w = a["w_in_2"][0]
    for j in range(2):
        put(START["sq"] + j, w[:, 2056 + 256 * j:2312 + 256 * j])
        put(START["z"] + j, w[:, 1536 + 256 * j:1792 + 256 * j])
    k0, k1 = w[:, 2568:2632], w[:, 2632:2696]
    put(START["sk"], beside(k0, k0, k1, k1))
    put(START["sv_ba"], beside(w[:, 2696:2824], w[:, 2048:2056]))
    for j in range(6):
        put(START["qkv"] + j, w[:, 256 * j:256 * (j + 1)])
    for m in range(4):
        c = START["merge"] + 4 * m
        for i in range(2):
            g = 2824 + (2 * m + i) * P
            put(c + i, beside(w[:, g:g + P], w[:, g + D:g + D + P]))
        put(c + 2, a["w_branch_dn_2"][0][:, m * 256:(m + 1) * 256])
        put(c + 3, a["w_branch_swa_2"][0][:, m * 256:(m + 1) * 256])
    c, t0 = START["ffn_2"], 0
    for n in FF2_TILES:
        for t in range(t0, t0 + n):
            put(c, beside(a["w_gate_2"][0][:, t * P:(t + 1) * P], a["w_up_2"][0][:, t * P:(t + 1) * P]))
            c += 1
        for m in range(4):
            put(c, a["w_down_2"][0][t0 * P:(t0 + n) * P, m * 256:(m + 1) * 256])
            c += 1
        t0 += n

    vecs = np.zeros((P, N_VEC), np.float32)
    for name, v in (("mix_pre", "mix_pre_g"), ("mix_post", "mix_post_g"), ("ffn_pre", "ffn_pre_g"),
                    ("ffn_post", "ffn_post_g"), ("b_pw1", "conv_b_pw1"), ("b_dw", "conv_b_dw"),
                    ("ln_g", "conv_ln_g"), ("ln_b", "conv_ln_b"), ("b_pw2", "conv_b_pw2"),
                    ("q_norm", "mla_q_norm_g"), ("kv_in", "kv_in_g"), ("kv_norm", "kv_norm_g"),
                    ("attn_norm", "attn_norm_2"), ("dn_out", "dn_out_norm_2"), ("ffn_norm", "ffn_norm_2"),
                    ("w_dw", "conv_w_dw"), ("dn_conv", "dn_conv_2")):
        v = a[v].reshape(-1, P)
        vecs[:, VEC[name]:VEC[name] + v.shape[0]] = v.T
    for name, v in (("swa_q", "swa_q_norm_2"), ("swa_k", "swa_k_norm_2")):
        for i in range(2):
            vecs[i * SW_D:(i + 1) * SW_D, VEC[name]] = a[v][0]

    consts = np.zeros((P, N_CONST), np.float32)

    def const(name, m):
        consts[:, CONST_COLS[name][0]:CONST_COLS[name][1]] = m

    i, j = np.indices((P, P))
    same = i // DN_CH == j // DN_CH
    const("ident", i == j)
    const("ones", np.ones((P, P)))
    const("half_ones", i // SW_D == j // SW_D)
    levels = [(i // (2 * b) == j // (2 * b)) & (i // b % 2 == 1) & (j // b % 2 == 0) for b in (1, 2, 4, 8, 16, 32)]
    const("inv_mask", np.concatenate(levels, axis=1))
    const("decay_mask", np.where(same & (i > j), 0.0, BIG))
    const("decay_mask_t", np.where(same & (i <= j), 0.0, -BIG))
    const("tri", same & (i <= j))
    const("rev", same & (i > j))
    inv = (1.0 / (np.float32(ROPE_BASE) ** (np.arange(0, ROPE, 2, dtype=np.float32) / np.float32(ROPE)))).astype(np.float32)
    ang = (np.arange(SEQ, dtype=np.float32)[None, :] * inv[:, None]).astype(np.float32)
    tables = np.zeros((P, 3, SEQ), np.float32)
    half = ROPE // 2
    for r in range(P):
        q = r % ROPE
        tables[(r - q) + (q + half) % ROPE, 0, r] = -1.0 if q < half else 1.0
    tables[:, 1] = np.tile(np.cos(ang), (4, 1))
    tables[:, 2] = np.tile(np.sin(ang), (4, 1))
    dist = 2 * P - 1 - np.arange(RELW)
    near = np.maximum(dist, 1).astype(np.float32)
    exact = BUCKETS // 2
    far = exact + (np.log(near / np.float32(exact)) / np.float32(math.log(MAX_DIST / exact))
                   * np.float32(BUCKETS - exact)).astype(np.int32)
    bucket = np.where(dist < exact, np.maximum(dist, 0), np.minimum(far, BUCKETS - 1))
    inside = (dist >= 0) & (dist < P)
    onehot = np.zeros((BUCKETS + 1, RELW), np.float32)
    onehot[:BUCKETS] = (np.arange(BUCKETS)[:, None] == bucket[None, :]) & inside[None, :]
    onehot[BUCKETS] = np.where(inside, 0.0, -BIG)
    x = a["x"][0].T.reshape(DT, P, SEQ).transpose(1, 0, 2)
    return {"stream": stream, "vecs": vecs, "consts": consts, "x": np.ascontiguousarray(x),
            "tables": tables, "onehot": onehot, "rel_bias": a["rel_bias_2"], "a_log": a["dn_a_log_2"][0],
            "dt_bias": a["dn_dt_bias_2"][0], "sinks": a["swa_sinks_2"][0]}


def kernel(**inputs):
    import numpy as np
    import concourse.bacc as bacc
    from concourse.bass_utils import run_bass_kernel_spmd

    arrays = pack(inputs)
    nc = bacc.Bacc("TRN2", target_bir_lowering=False, num_devices=1)
    A = {n: nc.dram_tensor(n, v.shape, F32, kind="ExternalInput").ap() for n, v in arrays.items()}
    out = nc.dram_tensor("out", (P, DT, SEQ), F32, kind="ExternalOutput").ap()
    build(nc, A, out)
    got = run_bass_kernel_spmd(nc, [arrays], core_ids=[0]).results[0]["out"]
    return np.ascontiguousarray(got.transpose(2, 1, 0).reshape(1, SEQ, D))
```
